# Optimizing a Trainium2 kernel written in Bass

```python
import jax, jax.numpy as jnp
from jax import lax
import numpy as np

D_MODEL = 2048
BATCH = 1
SEQ = 256
DEPTH = 1

FOX_HEADS = 8
FOX_HEAD_DIM = 128
FOX_WIDTH = FOX_HEADS * FOX_HEAD_DIM
NSA_HEADS = 8
NSA_KV_GROUPS = 2
NSA_HPG = NSA_HEADS // NSA_KV_GROUPS
NSA_QK_DIM = 192
NSA_V_DIM = 128
NSA_WIDTH = NSA_HEADS * NSA_V_DIM
CMP_BLOCK = 32
CMP_STRIDE = 16
CMP_HIDDEN = 256
SEL_BLOCK = 64
SEL_TOPK = 16
SEL_LOCAL = 2
FORCE_SCORE = 1.0e4
WINDOW = 512
Q_BLOCK = 128
SEL_Q_CHUNK = 32
KV_K = NSA_KV_GROUPS * NSA_QK_DIM
KV_V = NSA_KV_GROUPS * NSA_V_DIM
D_FF = -(-(8 * D_MODEL) // (3 * 256)) * 256
RMS_EPS = 1e-6
IN_SPLITS = (FOX_WIDTH, FOX_WIDTH, FOX_WIDTH, FOX_HEADS,
             NSA_HEADS * NSA_QK_DIM, KV_K, KV_V, KV_K, KV_V, KV_K, KV_V,
             3 * NSA_HEADS, D_MODEL, D_MODEL)
D_IN = sum(IN_SPLITS)


def _rms(x, gain):
    xf = x.astype(jnp.float32)
    y = xf * lax.rsqrt(jnp.mean(xf * xf, axis=-1, keepdims=True) + RMS_EPS)
    return (y * gain.astype(jnp.float32)).astype(x.dtype)

def _masked_softmax(s, mask):
    s = jnp.where(mask, s, -jnp.inf)
    m = jnp.max(s, axis=-1, keepdims=True)
    m = jnp.where(jnp.isfinite(m), m, 0.0)
    e = jnp.where(mask, jnp.exp(s - m), 0.0)
    return e / jnp.maximum(jnp.sum(e, axis=-1, keepdims=True), 1e-30)

def _alibi_slopes(n):
    return jnp.exp2(-8.0 * jnp.arange(1, n + 1, dtype=jnp.float32) / n)

def _fox_attention(q, k, v, log_f):
    B, T, H, Dh = q.shape
    nb = T // Q_BLOCK
    c = jnp.cumsum(log_f, axis=1).transpose(0, 2, 1)
    kh = k.transpose(0, 2, 1, 3)
    vh = v.transpose(0, 2, 1, 3)
    qb = q.reshape(B, nb, Q_BLOCK, H, Dh).transpose(1, 0, 3, 2, 4)
    cb = c.reshape(B, H, nb, Q_BLOCK).transpose(2, 0, 1, 3)
    scale = Dh ** -0.5
    kpos = jnp.arange(T)

    def block(args):
        qi, ci, i = args
        qpos = i * Q_BLOCK + jnp.arange(Q_BLOCK)
        s = jnp.einsum('bhqd,bhkd->bhqk', qi, kh, preferred_element_type=jnp.float32) * scale
        s = s + ci[..., :, None] - c[:, :, None, :]
        p = _masked_softmax(s, kpos[None, :] <= qpos[:, None])
        return jnp.einsum('bhqk,bhkd->bhqd', p.astype(vh.dtype), vh)

    o = lax.map(block, (qb, cb, jnp.arange(nb)))
    return o.transpose(1, 0, 3, 2, 4).reshape(B, T, H * Dh)

def _compress(z, pe, w1, w2):
    B, T, G, D = z.shape
    r = CMP_BLOCK // CMP_STRIDE
    ch = z.reshape(B, T // CMP_STRIDE, CMP_STRIDE, G, D)
    nc = T // CMP_STRIDE - r + 1
    blk = jnp.concatenate([ch[:, i:i + nc] for i in range(r)], axis=2)
    blk = blk + pe[None, None, :, None, :]
    flat = blk.transpose(0, 1, 3, 2, 4).reshape(B, nc, G, CMP_BLOCK * D)
    return jax.nn.silu(flat @ w1) @ w2

def _overlap_matrix(nc, ns):
    i = np.arange(nc)[:, None]
    j = np.arange(ns)[None, :]
    lo = np.maximum(i * CMP_STRIDE, j * SEL_BLOCK)
    hi = np.minimum(i * CMP_STRIDE + CMP_BLOCK, (j + 1) * SEL_BLOCK)
    return (np.maximum(hi - lo, 0) / CMP_STRIDE).astype(np.float32)

def _nsa_attention(q, kc_raw, vc_raw, ks_raw, vs_raw, kw_raw, vw_raw, gate_logits,
                   q_gain, kc_gain, ks_gain, kw_gain,
                   cmp_pe_k, cmp_w1_k, cmp_w2_k, cmp_pe_v, cmp_w1_v, cmp_w2_v):
    B, T, _ = q.shape
    G, HPG, Dk, Dv = NSA_KV_GROUPS, NSA_HPG, NSA_QK_DIM, NSA_V_DIM
    scale = Dk ** -0.5
    slopes = _alibi_slopes(NSA_HEADS).reshape(G, HPG)
    tpos = jnp.arange(T)
    qn = _rms(q.reshape(B, T, G, HPG, Dk), q_gain)
    qc = qn.transpose(0, 2, 3, 1, 4)

    kc = _rms(_compress(kc_raw.reshape(B, T, G, Dk), cmp_pe_k, cmp_w1_k, cmp_w2_k), kc_gain)
    vc = _compress(vc_raw.reshape(B, T, G, Dv), cmp_pe_v, cmp_w1_v, cmp_w2_v)
    nc = kc.shape[1]
    cend = jnp.arange(nc) * CMP_STRIDE + CMP_BLOCK - 1
    dist_c = tpos[:, None] - cend[None, :]
    s_c = jnp.einsum('btghd,bngd->bghtn', qn, kc, preferred_element_type=jnp.float32) * scale
    s_c = s_c - slopes[None, :, :, None, None] * dist_c.astype(jnp.float32)
    p_cmp = _masked_softmax(s_c, dist_c >= 0)
    o_cmp = jnp.einsum('bghtn,bngd->btghd', p_cmp.astype(vc.dtype), vc)

    ns = T // SEL_BLOCK
    n_sel = min(SEL_TOPK, ns)
    imp = jnp.einsum('bgtn,nj->bgtj', p_cmp.sum(axis=2), jnp.asarray(_overlap_matrix(nc, ns)))
    cur = tpos // SEL_BLOCK
    jidx = jnp.arange(ns)
    back = cur[:, None] - jidx[None, :]
    eligible = back >= 0
    forced = (jidx[None, :] == 0) | (eligible & (back < SEL_LOCAL))
    score = jnp.where(eligible, jnp.where(forced, FORCE_SCORE, imp), -1.0)
    top_score, idx = lax.top_k(score, n_sel)
    valid = top_score >= 0.0

    ks_b = _rms(ks_raw.reshape(B, T, G, Dk), ks_gain).transpose(0, 2, 1, 3).reshape(B, G, ns, SEL_BLOCK, Dk)
    vs_b = vs_raw.reshape(B, T, G, Dv).transpose(0, 2, 1, 3).reshape(B, G, ns, SEL_BLOCK, Dv)
    nq = T // SEL_Q_CHUNK
    q_ch = qc.reshape(B, G, HPG, nq, SEL_Q_CHUNK, Dk).transpose(3, 0, 1, 2, 4, 5)
    idx_ch = idx.reshape(B, G, nq, SEL_Q_CHUNK, n_sel).transpose(2, 0, 1, 3, 4)
    val_ch = valid.reshape(B, G, nq, SEL_Q_CHUNK, n_sel).transpose(2, 0, 1, 3, 4)
    bi = jnp.arange(B)[:, None, None, None]
    gi = jnp.arange(G)[None, :, None, None]
    in_blk = jnp.arange(SEL_BLOCK)

    def sel_chunk(args):
        qi, ii, vi, c = args
        kg = ks_b[bi, gi, ii]
        vg = vs_b[bi, gi, ii].reshape(B, G, SEL_Q_CHUNK, n_sel * SEL_BLOCK, Dv)
        qpos = c * SEL_Q_CHUNK + jnp.arange(SEL_Q_CHUNK)
        kpos = ii[..., None] * SEL_BLOCK + in_blk
        dist = qpos[None, None, :, None, None] - kpos
        mask = ((dist >= 0) & vi[..., None]).reshape(B, G, 1, SEL_Q_CHUNK, n_sel * SEL_BLOCK)
        s = jnp.einsum('bghqd,bgqskd->bghqsk', qi, kg, preferred_element_type=jnp.float32) * scale
        s = s - slopes[None, :, :, None, None, None] * dist[:, :, None].astype(jnp.float32)
        p = _masked_softmax(s.reshape(B, G, HPG, SEL_Q_CHUNK, n_sel * SEL_BLOCK), mask)
        return jnp.einsum('bghqk,bgqkd->bghqd', p.astype(vg.dtype), vg)

    o_slc = lax.map(sel_chunk, (q_ch, idx_ch, val_ch, jnp.arange(nq)))
    o_slc = o_slc.transpose(1, 0, 4, 2, 3, 5).reshape(B, T, G, HPG, Dv)

    nb = T // Q_BLOCK
    r = WINDOW // Q_BLOCK
    kw = _rms(kw_raw.reshape(B, T, G, Dk), kw_gain).transpose(0, 2, 1, 3)
    vw = vw_raw.reshape(B, T, G, Dv).transpose(0, 2, 1, 3)
    pad = ((0, 0), (0, 0), (WINDOW, 0), (0, 0))
    kwb = jnp.pad(kw, pad).reshape(B, G, nb + r, Q_BLOCK, Dk)
    vwb = jnp.pad(vw, pad).reshape(B, G, nb + r, Q_BLOCK, Dv)
    band_k = jnp.concatenate([kwb[:, :, i:i + nb] for i in range(r + 1)], axis=3)
    band_v = jnp.concatenate([vwb[:, :, i:i + nb] for i in range(r + 1)], axis=3)
    kb_len = (r + 1) * Q_BLOCK
    dist_w = jnp.arange(Q_BLOCK)[:, None] - jnp.arange(kb_len)[None, :] + WINDOW
    kpos_w = jnp.arange(nb)[:, None] * Q_BLOCK - WINDOW + jnp.arange(kb_len)[None, :]
    mask_w = (dist_w >= 0)[None] & (dist_w < WINDOW)[None] & (kpos_w >= 0)[:, None, :]
    q_w = qc.reshape(B, G, HPG, nb, Q_BLOCK, Dk)
    s_w = jnp.einsum('bghnqd,bgnkd->bghnqk', q_w, band_k, preferred_element_type=jnp.float32) * scale
    s_w = s_w - slopes[None, :, :, None, None, None] * dist_w.astype(jnp.float32)
    p_w = _masked_softmax(s_w, mask_w)
    o_win = jnp.einsum('bghnqk,bgnkd->bghnqd', p_w.astype(band_v.dtype), band_v)
    o_win = o_win.reshape(B, G, HPG, T, Dv).transpose(0, 3, 1, 2, 4)

    g = jax.nn.sigmoid(gate_logits.astype(jnp.float32)).reshape(B, T, G, HPG, 3)
    o = g[..., 0:1] * o_cmp + g[..., 1:2] * o_slc + g[..., 2:3] * o_win
    return o.reshape(B, T, NSA_WIDTH).astype(q.dtype)

def first_inputs(seed: int = 0) -> dict:
    key = jax.random.key(seed)
    ks = jax.random.split(key, 24)
    f32 = jnp.float32
    L = DEPTH

    def nrm(k, shape, fan_in):
        return jax.random.normal(k, shape, f32) * fan_in ** -0.5

    def gain(k, shape):
        return 1.0 + 0.02 * jax.random.normal(k, shape, f32)

    return {
        "x": jax.random.normal(ks[0], (BATCH, SEQ, D_MODEL), f32),
        "norm_attn": gain(ks[1], (L, D_MODEL)),
        "w_in": nrm(ks[2], (L, D_MODEL, D_IN), D_MODEL),
        "fox_f_bias": 3.0 + 0.1 * jax.random.normal(ks[3], (L, FOX_HEADS), f32),
        "fox_q_gain": gain(ks[4], (L, FOX_HEAD_DIM)),
        "fox_k_gain": gain(ks[5], (L, FOX_HEAD_DIM)),
        "nsa_q_gain": gain(ks[6], (L, NSA_QK_DIM)),
        "nsa_kc_gain": gain(ks[7], (L, NSA_QK_DIM)),
        "nsa_ks_gain": gain(ks[8], (L, NSA_QK_DIM)),
        "nsa_kw_gain": gain(ks[9], (L, NSA_QK_DIM)),
        "cmp_pe_k": 0.02 * jax.random.normal(ks[10], (L, CMP_BLOCK, NSA_QK_DIM), f32),
        "cmp_w1_k": nrm(ks[11], (L, CMP_BLOCK * NSA_QK_DIM, CMP_HIDDEN), CMP_BLOCK * NSA_QK_DIM),
        "cmp_w2_k": nrm(ks[12], (L, CMP_HIDDEN, NSA_QK_DIM), CMP_HIDDEN),
        "cmp_pe_v": 0.02 * jax.random.normal(ks[13], (L, CMP_BLOCK, NSA_V_DIM), f32),
        "cmp_w1_v": nrm(ks[14], (L, CMP_BLOCK * NSA_V_DIM, CMP_HIDDEN), CMP_BLOCK * NSA_V_DIM),
        "cmp_w2_v": nrm(ks[15], (L, CMP_HIDDEN, NSA_V_DIM), CMP_HIDDEN),
        "w_up_fox": nrm(ks[16], (L, FOX_WIDTH, D_MODEL), FOX_WIDTH),
        "w_up_nsa": nrm(ks[17], (L, NSA_WIDTH, D_MODEL), NSA_WIDTH),
        "w_out": nrm(ks[18], (L, D_MODEL, D_MODEL), D_MODEL),
        "norm_ffn": gain(ks[19], (L, D_MODEL)),
        "w_ffn_gate": nrm(ks[20], (L, D_MODEL, D_FF), D_MODEL),
        "w_ffn_up": nrm(ks[21], (L, D_MODEL, D_FF), D_MODEL),
        "w_ffn_down": nrm(ks[22], (L, D_FF, D_MODEL), D_FF),
    }

def first_block(x, norm_attn, w_in, fox_f_bias, fox_q_gain, fox_k_gain,
              nsa_q_gain, nsa_kc_gain, nsa_ks_gain, nsa_kw_gain,
              cmp_pe_k, cmp_w1_k, cmp_w2_k, cmp_pe_v, cmp_w1_v, cmp_w2_v,
              w_up_fox, w_up_nsa, w_out, norm_ffn, w_ffn_gate, w_ffn_up, w_ffn_down):
    B, T, _ = x.shape
    points = tuple(int(p) for p in np.cumsum(IN_SPLITS)[:-1])
    for l in range(DEPTH):
        xn = _rms(x, norm_attn[l])
        (fq, fk, fv, f_logit, nq, kc, vc, ksl, vsl, kw, vw,
         nsa_gate, gate_a, gate_b) = jnp.split(xn @ w_in[l], points, axis=-1)

        fq = _rms(fq.reshape(B, T, FOX_HEADS, FOX_HEAD_DIM), fox_q_gain[l])
        fk = _rms(fk.reshape(B, T, FOX_HEADS, FOX_HEAD_DIM), fox_k_gain[l])
        fv = fv.reshape(B, T, FOX_HEADS, FOX_HEAD_DIM)
        log_f = jax.nn.log_sigmoid(f_logit.astype(jnp.float32) + fox_f_bias[l].astype(jnp.float32))
        o_a = _fox_attention(fq, fk, fv, log_f)

        o_b = _nsa_attention(nq, kc, vc, ksl, vsl, kw, vw, nsa_gate,
                             nsa_q_gain[l], nsa_kc_gain[l], nsa_ks_gain[l], nsa_kw_gain[l],
                             cmp_pe_k[l], cmp_w1_k[l], cmp_w2_k[l],
                             cmp_pe_v[l], cmp_w1_v[l], cmp_w2_v[l])

        merged = (jax.nn.sigmoid(gate_a) * (o_a @ w_up_fox[l])
                  + jax.nn.sigmoid(gate_b) * (o_b @ w_up_nsa[l]))
        x = x + (merged @ w_out[l]).astype(x.dtype)

        hn = _rms(x, norm_ffn[l])
        x = x + ((jax.nn.silu(hn @ w_ffn_gate[l]) * (hn @ w_ffn_up[l])) @ w_ffn_down[l]).astype(x.dtype)
    return x


DEPTH_2 = 2

N_MIXERS = 2
GRID_W = 64
N_META = 16
NORM_EPS = 1e-6

ATTN_HEADS = 16
ATTN_KV_HEADS = 8
ATTN_GROUP = ATTN_HEADS // ATTN_KV_HEADS
ATTN_HEAD_DIM = 128
ATTN_WIDTH = ATTN_HEADS * ATTN_HEAD_DIM
ATTN_KV_WIDTH = ATTN_KV_HEADS * ATTN_HEAD_DIM
ATTN_IN = 2 * ATTN_WIDTH + 2 * ATTN_KV_WIDTH
ROPE_THETA = 10000.0
ROPE_AXIS_DIM = ATTN_HEAD_DIM // 2

GLA_HEADS = 4
GLA_KEY_DIM = D_MODEL // 2
GLA_VALUE_DIM = D_MODEL
GLA_HEAD_K = GLA_KEY_DIM // GLA_HEADS
GLA_HEAD_V = GLA_VALUE_DIM // GLA_HEADS
GLA_GATE_RANK = 16
GLA_GATE_NORMALIZER = 16.0
GLA_CHUNK = 64
GLA_IN = 2 * GLA_KEY_DIM + 2 * GLA_VALUE_DIM + 2 * GLA_GATE_RANK

N_ATTN_LAYERS = (DEPTH_2 + 1) // 2
N_GLA_LAYERS = DEPTH_2 // 2


def rmsnorm(x, w):
    xf = x.astype(jnp.float32)
    y = xf * lax.rsqrt(jnp.mean(xf * xf, axis=-1, keepdims=True) + NORM_EPS)
    return (y * w.astype(jnp.float32)).astype(x.dtype)

def axial_rope_angles(seq_len):
    rows = seq_len // GRID_W
    row = jnp.repeat(jnp.arange(rows), GRID_W).astype(jnp.float32)
    col = jnp.tile(jnp.arange(GRID_W), rows).astype(jnp.float32)
    inv_freq = ROPE_THETA ** (-jnp.arange(0, ROPE_AXIS_DIM, 2, dtype=jnp.float32) / ROPE_AXIS_DIM)
    meta = jnp.zeros((N_META, ROPE_AXIS_DIM // 2), jnp.float32)
    ang_row = jnp.concatenate([meta, row[:, None] * inv_freq[None]], axis=0)
    ang_col = jnp.concatenate([meta, col[:, None] * inv_freq[None]], axis=0)
    return ang_row, ang_col

def _rotate(x, ang):
    cos = jnp.cos(ang)[None, :, None, :].astype(x.dtype)
    sin = jnp.sin(ang)[None, :, None, :].astype(x.dtype)
    x1, x2 = jnp.split(x, 2, axis=-1)
    return jnp.concatenate([x1 * cos - x2 * sin, x2 * cos + x1 * sin], axis=-1)

def apply_axial_rope(x, ang_row, ang_col):
    return jnp.concatenate([_rotate(x[..., :ROPE_AXIS_DIM], ang_row),
                            _rotate(x[..., ROPE_AXIS_DIM:], ang_col)], axis=-1)

def _attend(qb, k, v):
    s = jnp.einsum('bqkgd,bskd->bkgqs', qb, k) * (ATTN_HEAD_DIM ** -0.5)
    p = jax.nn.softmax(s.astype(jnp.float32), axis=-1).astype(v.dtype)
    return jnp.einsum('bkgqs,bskd->bqkgd', p, v)

def attention_mixer(h, w_in, q_norm, k_norm, w_out, ang_row, ang_col):
    B, L, _ = h.shape
    proj = h @ w_in
    q, k, v, gate = jnp.split(
        proj, [ATTN_WIDTH, ATTN_WIDTH + ATTN_KV_WIDTH, ATTN_WIDTH + 2 * ATTN_KV_WIDTH], axis=-1)
    q = q.reshape(B, L, ATTN_HEADS, ATTN_HEAD_DIM)
    k = k.reshape(B, L, ATTN_KV_HEADS, ATTN_HEAD_DIM)
    v = v.reshape(B, L, ATTN_KV_HEADS, ATTN_HEAD_DIM)
    q = apply_axial_rope(rmsnorm(q, q_norm), ang_row, ang_col)
    k = apply_axial_rope(rmsnorm(k, k_norm), ang_row, ang_col)
    q = q.reshape(B, L, ATTN_KV_HEADS, ATTN_GROUP, ATTN_HEAD_DIM)
    o_meta = _attend(q[:, :N_META], k, v)
    n_real = L - N_META
    nb = n_real // Q_BLOCK
    q_blocks = q[:, N_META:].reshape(B, nb, Q_BLOCK, ATTN_KV_HEADS, ATTN_GROUP, ATTN_HEAD_DIM)
    o_real = lax.map(lambda qb: _attend(qb, k, v), jnp.swapaxes(q_blocks, 0, 1))
    o_real = jnp.swapaxes(o_real, 0, 1).reshape(B, n_real, ATTN_KV_HEADS, ATTN_GROUP, ATTN_HEAD_DIM)
    o = jnp.concatenate([o_meta, o_real], axis=1).reshape(B, L, ATTN_WIDTH)
    return (o * jax.nn.silu(gate)) @ w_out

def gla_chunked(q, k, v, g, strict):
    B, H, T, dk = q.shape
    dv = v.shape[-1]
    n = T // GLA_CHUNK

    def chunks(t):
        return t.reshape(B, H, n, GLA_CHUNK, t.shape[-1]).astype(jnp.float32)

    qc, kc, vc, gc = chunks(q), chunks(k), chunks(v), chunks(g)
    b = jnp.cumsum(gc, axis=3)
    b_last = b[:, :, :, -1:, :]
    q_dec = qc * jnp.exp(b)
    k_inv = kc * jnp.exp(-b)
    k_end = kc * jnp.exp(b_last - b)
    scores = jnp.einsum('bhncd,bhnsd->bhncs', q_dec, k_inv)
    mask = jnp.tril(jnp.ones((GLA_CHUNK, GLA_CHUNK), bool), k=-1 if strict else 0)
    o_intra = jnp.einsum('bhncs,bhnse->bhnce', jnp.where(mask, scores, 0.0), vc)

    def step(S, xs):
        q_t, k_t, v_t, dl = xs
        o = jnp.einsum('bhcd,bhde->bhce', q_t, S)
        S = S * dl[..., None] + jnp.einsum('bhcd,bhce->bhde', k_t, v_t)
        return S, o

    xs = (jnp.moveaxis(q_dec, 2, 0), jnp.moveaxis(k_end, 2, 0), jnp.moveaxis(vc, 2, 0),
          jnp.moveaxis(jnp.exp(b_last[:, :, :, 0, :]), 2, 0))
    S0 = jnp.zeros((B, H, dk, dv), jnp.float32)
    _, o_inter = lax.scan(step, S0, xs)
    o = o_intra + jnp.moveaxis(o_inter, 0, 2)
    return o.reshape(B, H, T, dv).astype(q.dtype)

def gla_mixer(h, w_in, gk_up, gk_bias, o_norm, w_out):
    B, L, _ = h.shape
    pad = GLA_CHUNK - N_META
    hp = jnp.pad(h, ((0, 0), (pad, 0), (0, 0)))
    T = L + pad
    proj = hp @ w_in
    s1 = GLA_KEY_DIM
    s2 = s1 + GLA_KEY_DIM
    s3 = s2 + GLA_VALUE_DIM
    s4 = s3 + GLA_VALUE_DIM
    s5 = s4 + GLA_GATE_RANK
    q, k, v, g_out, lr_f, lr_b = jnp.split(proj, [s1, s2, s3, s4, s5], axis=-1)

    def heads(t, d):
        return t.reshape(B, T, GLA_HEADS, d).transpose(0, 2, 1, 3)

    def log_gate(lr, up, bias):
        z = (lr @ up + bias).astype(jnp.float32)
        return heads(jax.nn.log_sigmoid(z) / GLA_GATE_NORMALIZER, GLA_HEAD_K)

    q = heads(q, GLA_HEAD_K) * (GLA_HEAD_K ** -0.5)
    k = heads(k, GLA_HEAD_K)
    v = heads(v, GLA_HEAD_V)
    flip = lambda t: jnp.flip(t, axis=2)
    o_f = gla_chunked(q, k, v, log_gate(lr_f, gk_up[0], gk_bias[0]), strict=False)
    o_b = flip(gla_chunked(flip(q), flip(k), flip(v),
                           flip(log_gate(lr_b, gk_up[1], gk_bias[1])), strict=True))
    o = (o_f + o_b).transpose(0, 2, 1, 3)[:, pad:]
    o = rmsnorm(o, o_norm).reshape(B, L, GLA_VALUE_DIM)
    return (o * jax.nn.silu(g_out[:, pad:])) @ w_out

def second_inputs(seed: int = 0) -> dict:
    key = jax.random.key(seed)
    ks = jax.random.split(key, 13)
    f32 = jnp.float32
    nrm = lambda k, shape, scale: jax.random.normal(k, shape, f32) * scale
    return {
        "x": nrm(ks[0], (BATCH, SEQ, D_MODEL), 1.0),
        "meta_tokens": nrm(ks[1], (N_META, D_MODEL), 1.0),
        "pre_norm": 1.0 + nrm(ks[2], (DEPTH_2, D_MODEL), 0.02),
        "post_norm": 1.0 + nrm(ks[3], (DEPTH_2, D_MODEL), 0.02),
        "attn_w_in": nrm(ks[4], (N_ATTN_LAYERS, D_MODEL, ATTN_IN), D_MODEL ** -0.5),
        "attn_q_norm": 1.0 + nrm(ks[5], (N_ATTN_LAYERS, ATTN_HEAD_DIM), 0.02),
        "attn_k_norm": 1.0 + nrm(ks[6], (N_ATTN_LAYERS, ATTN_HEAD_DIM), 0.02),
        "attn_w_out": nrm(ks[7], (N_ATTN_LAYERS, ATTN_WIDTH, D_MODEL), ATTN_WIDTH ** -0.5),
        "gla_w_in": nrm(ks[8], (N_GLA_LAYERS, D_MODEL, GLA_IN), D_MODEL ** -0.5),
        "gla_gk_up": nrm(ks[9], (N_GLA_LAYERS, 2, GLA_GATE_RANK, GLA_KEY_DIM), GLA_GATE_RANK ** -0.5),
        "gla_gk_bias": nrm(ks[10], (N_GLA_LAYERS, 2, GLA_KEY_DIM), 0.1),
        "gla_o_norm": 1.0 + nrm(ks[11], (N_GLA_LAYERS, GLA_HEAD_V), 0.02),
        "gla_w_out": nrm(ks[12], (N_GLA_LAYERS, GLA_VALUE_DIM, D_MODEL), GLA_VALUE_DIM ** -0.5),
    }

def second_block(x, meta_tokens, pre_norm, post_norm, attn_w_in, attn_q_norm, attn_k_norm,
              attn_w_out, gla_w_in, gla_gk_up, gla_gk_bias, gla_o_norm, gla_w_out):
    B, S, D = x.shape
    meta = jnp.broadcast_to(meta_tokens.astype(x.dtype)[None], (B, N_META, D))
    h = jnp.concatenate([meta, x], axis=1)
    ang_row, ang_col = axial_rope_angles(S)
    for i in range(DEPTH_2):
        y = rmsnorm(h, pre_norm[i])
        j = i // N_MIXERS
        if i % N_MIXERS == 0:
            y = attention_mixer(y, attn_w_in[j], attn_q_norm[j], attn_k_norm[j], attn_w_out[j],
                                ang_row, ang_col)
        else:
            y = gla_mixer(y, gla_w_in[j], gla_gk_up[j], gla_gk_bias[j], gla_o_norm[j], gla_w_out[j])
        h = h + rmsnorm(y, post_norm[i])
    return h[:, N_META:]


def setup_inputs(seed=0):
    out = dict(first_inputs(seed))
    for name, value in second_inputs(seed + 1).items():
        if name != "x":
            out[name + "_2"] = value
    return out


def reference(
    x, norm_attn, w_in, fox_f_bias, fox_q_gain, fox_k_gain, nsa_q_gain, nsa_kc_gain,
    nsa_ks_gain, nsa_kw_gain, cmp_pe_k, cmp_w1_k, cmp_w2_k, cmp_pe_v, cmp_w1_v, cmp_w2_v,
    w_up_fox, w_up_nsa, w_out, norm_ffn, w_ffn_gate, w_ffn_up, w_ffn_down, meta_tokens_2,
    pre_norm_2, post_norm_2, attn_w_in_2, attn_q_norm_2, attn_k_norm_2, attn_w_out_2,
    gla_w_in_2, gla_gk_up_2, gla_gk_bias_2, gla_o_norm_2, gla_w_out_2,
):
    x = first_block(
        x, norm_attn, w_in, fox_f_bias, fox_q_gain, fox_k_gain, nsa_q_gain, nsa_kc_gain,
        nsa_ks_gain, nsa_kw_gain, cmp_pe_k, cmp_w1_k, cmp_w2_k, cmp_pe_v, cmp_w1_v, cmp_w2_v,
        w_up_fox, w_up_nsa, w_out, norm_ffn, w_ffn_gate, w_ffn_up, w_ffn_down,
    )
    return second_block(
        x, meta_tokens_2, pre_norm_2, post_norm_2, attn_w_in_2, attn_q_norm_2, attn_k_norm_2,
        attn_w_out_2, gla_w_in_2, gla_gk_up_2, gla_gk_bias_2, gla_o_norm_2, gla_w_out_2,
    )


_drawn_inputs = setup_inputs


def setup_inputs(seed=0):
    import zlib

    import numpy as np

    out = dict(_drawn_inputs(seed))
    spreads = {}
    factors = {'norm_attn': 3.102,
     'fox_q_gain': 8.0,
     'fox_k_gain': 8.0,
     'nsa_q_gain': 8.0,
     'nsa_kc_gain': 8.0,
     'nsa_ks_gain': 8.0,
     'nsa_kw_gain': 8.0,
     'cmp_pe_k': 8.0,
     'cmp_pe_v': 13.917,
     'attn_q_norm_2': 3.354,
     'attn_k_norm_2': 3.546,
     'gla_o_norm_2': 200.0,
     'norm_ffn': 4.415,
     'post_norm_2': 27.699,
     'gla_gk_bias_2': 4.111}
    for name, (base, spread) in spreads.items():
        noise = np.random.default_rng([zlib.crc32(name.encode()), seed]).standard_normal(out[name].shape)
        drawn = base * np.exp(spread * noise) if base else spread * noise
        out[name] = __import__('jax').numpy.asarray(drawn.astype(out[name].dtype))
    for name, factor in factors.items():
        out[name] = (out[name] * factor).astype(out[name].dtype)
    return out
```

```python
from contextlib import ExitStack

import numpy as np
import concourse.bass as bass
from concourse import mybir

P = 128
T = 256
META = 16
TM = T + META
D = 2048
KC = D // P
HB = KC // 2
D_FF = 5632
FOX_H, FOX_D = 8, 128
NSA_H, NSA_G, NSA_DK, NSA_DV = 8, 2, 192, 128
NB_C = 15
GQ_KV, GQ_D = 8, 128
GLA_H, GLA_C = 4, 64
EPS = 1e-6
SCRATCH = 2048
BIG = 1e30

F32 = mybir.dt.float32
F32R = mybir.dt.float32r
ALU = mybir.AluOpType
ACT = mybir.ActivationFunctionType
AX = mybir.AxisListType.X

C_FQ, C_FK, C_FV, C_F = 0, 1024, 2048, 3072
C_NQ, C_KC, C_VC = 3080, 4616, 5000
C_KS, C_VS, C_KW, C_VW = 5256, 5640, 5896, 6280
C_NG, C_GATES = 6536, 6560

U_B0 = 0
U_FOX = U_B0 + 2
U_NKV = U_FOX + 4 * FOX_H
U_NQ = U_NKV + 15
U_GATE = U_NQ + 4 * 4
U_UP = U_GATE + 20
U_OUT = U_UP + 16
U_FFN = U_OUT + 16

V_ATTN, V_FFN, V_PRE, V_POST, V_GKB = 0, 16, 32, 64, 96
V_FQ, V_FK, V_NQ, V_KC, V_KS, V_KW, V_AQ, V_AK, V_ON = 112, 113, 114, 115, 116, 117, 118, 119, 120
N_VA = 124
V_PEK, V_PEV, V_PET, V_TQ = 0, 32, 64, 96
N_VB = 100

K_ID, K_TRI, K_ONE, K_I128, K_I192, K_ID2048, K_DIST, K_DISTC, K_MASKC, K_SLOPE, K_EPS = (
    0, 128, 384, 640, 768, 896, 1024, 1280, 1310, 1340, 1348)
N_K = 1349
N_K2 = 2 * T + 3 * P


def shape_constants():
    k = np.zeros((P, N_K + N_K2), np.float32)
    q = np.arange(P)[:, None]
    k[:, K_ID:K_ID + P] = np.eye(P)
    kk = np.arange(T)[None, :]
    k[:, K_TRI:K_TRI + T] = np.where(kk <= q + P, 0.0, BIG)
    k[:, K_ONE:K_ONE + T] = 1.0
    k[:, K_I128:K_I128 + P] = 1.0 / 128
    k[:, K_I192:K_I192 + P] = np.float32(1.0) / np.float32(192)
    k[:, K_ID2048:K_ID2048 + P] = 1.0 / 2048
    k[:, K_DIST:K_DIST + T] = np.where(kk <= q + P, q + P - kk, BIG)
    t = q[:, :, None] + P * np.arange(2)[None, :, None]
    dist = t - (16 * np.arange(NB_C) + 31)[None, None, :]
    k[:, K_DISTC:K_DISTC + 30] = np.where(dist >= 0, dist, BIG).reshape(P, 30)
    k[:, K_MASKC:K_MASKC + 30] = (dist >= 0).reshape(P, 30)
    k[:, K_SLOPE:K_SLOPE + NSA_H] = 2.0 ** -(np.arange(NSA_H) + 1.0)
    k[:, K_EPS] = EPS
    d = np.arange(P)
    freq = np.float32(10000.0) ** (-(2 * (d % 32)) / np.float32(64)).astype(np.float32)
    pos = np.where(d[:, None] < 64, kk // 64, kk % 64).astype(np.float32)
    angle = (pos * freq[:, None]).astype(np.float32)
    k[:, N_K:N_K + T] = np.cos(angle)
    k[:, N_K + T:N_K + 2 * T] = np.sin(angle) * np.where(d % 64 < 32, -1, 1)[:, None]
    k[d, N_K + 2 * T + (d ^ 32)] = 1.0
    k[:, N_K + 2 * T + P:N_K + 2 * T + 2 * P] = d[:, None] <= d[None, :]
    k[:, N_K + 2 * T + 2 * P:] = d[:, None] > d[None, :]
    return k


class Chain:

    def __init__(self, eng, sem):
        self.eng, self.sem, self.n, self.at = eng, sem, 0, 0

    def begin(self, i, per, base):
        self.at, self.n, self.per = base + per * i, 0, per

    def link(self, ins):
        self.n += 1
        ins.then_inc(self.sem, 1)
        self.eng.wait_ge(self.sem, self.at + self.n)

    def end(self):
        assert self.n == self.per, (self.n, self.per)


def program(nc, a, const, out):
    with ExitStack() as ctx:
        def sb(name, shape, dt=F32):
            return ctx.enter_context(nc.sbuf_tensor(name, shape, dt))

        def bank(name):
            return ctx.enter_context(nc.psum_tensor(name, [P, 512], F32))

        def sem(name):
            return ctx.enter_context(nc.semaphore(name))

        raw = sb("raw", [P, 8, HB * P])
        hi = sb("w_hi", [P, 4, HB * P], F32R)
        lo = sb("w_lo", [P, 4, HB * P], F32R)
        raw_full = [sem(f"raw_full{n}") for n in range(8)]
        tail_full = [sem(f"tail_full{n}") for n in range(8)]
        hi_ready, lo_ready = sem("hi_ready"), sem("lo_ready")
        block_done, evacuated = sem("block_done"), sem("evacuated")

        X = sb("x_res", [P, KC, TM])
        AH, AL = sb("a_hi", [P, KC, TM], F32R), sb("a_lo", [P, KC, TM], F32R)
        BH, BL = sb("b_hi", [P, KC, TM], F32R), sb("b_lo", [P, KC, TM], F32R)
        G = sb("g_buf", [P, 2 * KC * TM])
        con = sb("con", [P, N_K])
        VA = sb("vec_a", [P, N_VA])
        VB = sb("vec_b", [P, N_VB])
        RS = sb("rms", [P, TM])
        W = sb("work", [P, 7936])
        ACC = W[:, 7120:7392]
        SQ = W[:, 7392:7936].rearrange("p (a n) -> p a n", a=2)

        ident = con[:, K_ID:K_ID + P]
        ones = con[:, K_ONE:K_ONE + T]
        tri = con[:, K_TRI:K_TRI + T]
        i128, i192, i2048 = (con[:, k:k + P] for k in (K_I128, K_I192, K_ID2048))

        psU = [bank("ps_unit0"), bank("ps_unit1")]
        psS = [bank("ps_score0"), bank("ps_score1")]
        psT = [bank("ps_turn0"), bank("ps_turn1")]
        psN, psO = bank("ps_norm"), bank("ps_out")

        w_in = a["w_in"][0].rearrange("(k p) n -> p k n", p=P)

        def ch(x, kc, N):
            if isinstance(kc, int):
                return x[:, kc, 0:N]
            return x[:, bass.ds(kc, 1), 0:N].rearrange("p a n -> p (a n)")

        def gates(j):
            g = G[:, 0:32 * T].rearrange("p (a j n) -> p a j n", a=2, n=T)
            return g[:, :, bass.ds(j, 1), :].rearrange("p a b n -> p a (b n)")

        def load_block(eng, U, h, n, i, src, kb=HB, w=P, first=False):
            b = 2 * U + h
            if not first:
                eng.wait_ge(lo_ready, b + 2 * n * i - 7)
            eng.dma_start(raw[:, b % 8, 0:kb * w].rearrange("p (k m) -> p k m", m=w), src)\
               .then_inc(raw_full[b % 8], 16)

        def load_unit(eng, U, n, i, wv, c, kb=HB, w=P, first=False):
            for h in range(2):
                load_block(eng, U, h, n, i, wv[:, h * kb:(h + 1) * kb, bass.ds(c, w)], kb, w,
                           first and 2 * U + h < 8)

        def load_tails(eng, U, n, i, c):
            for h in range(2):
                b = 2 * U + h
                eng.wait_ge(lo_ready, b + 2 * n * i - 7)
                dst = raw[:, b % 8, :].rearrange("p (k g m) -> p k g m", g=2, m=64)
                src = w_in[:, h * HB:(h + 1) * HB, bass.ds(c, 2 * NSA_DK)]\
                    .rearrange("p k (g d) -> p k g d", g=2)[:, :, :, P:NSA_DK]
                eng.dma_start(dst[:, :, 0], src[:, :, 0]).then_inc(raw_full[b % 8], 16)
                eng.dma_start(dst[:, :, 1], src[:, :, 1]).then_inc(tail_full[b % 8], 16)

        def split_hi(act, U, n, i, size=HB * P, tails=None):
            for h in range(2):
                b = 2 * U + h
                act.wait_ge(raw_full[b % 8], 16 * (b // 8 + 1 + n // 4 * i))
                if tails is not None:
                    act.wait_ge(tail_full[b % 8], 16 * tails)
                if b >= 4:
                    act.wait_ge(block_done, b + 2 * n * i - 3)
                act.activation(hi[:, b % 4, 0:size], raw[:, b % 8, 0:size], ACT.Copy)\
                   .then_inc(hi_ready, 1)

        def split_lo(dve, U, n, i, size=HB * P):
            for h in range(2):
                b = 2 * U + h
                dve.wait_ge(hi_ready, b + 2 * n * i + 1)
                dve.tensor_tensor(lo[:, b % 4, 0:size], raw[:, b % 8, 0:size],
                                  hi[:, b % 4, 0:size], ALU.subtract).then_inc(lo_ready, 1)

        def mm_block(pe, U, h, n, i, xh, xl, k0, dst, N, kb=HB, w=P, start=True, stop=True):
            b = 2 * U + h
            pe.wait_ge(lo_ready, b + 2 * n * i + 1)
            if h == 0 and U >= 2:
                pe.wait_ge(evacuated, U + n * i - 1)
            for k in range(kb):
                wh = hi[:, b % 4, k * w:(k + 1) * w]
                wl = lo[:, b % 4, k * w:(k + 1) * w]
                pe.matmul(dst, wh, xh[:, k0 + k, 0:N], start=start and k == 0, stop=False)
                pe.matmul(dst, wh, xl[:, k0 + k, 0:N], start=False, stop=False)
                mm = pe.matmul(dst, wl, xh[:, k0 + k, 0:N], start=False,
                               stop=stop and k == kb - 1)
            mm.then_inc(block_done, 1)

        def mm_unit(pe, U, n, i, xh, xl, N=T, kb=HB, w=P):
            dst = psU[U % 2][0:w, 0:N]
            mm_block(pe, U, 0, n, i, xh, xl, 0, dst, N, kb, w, stop=False)
            mm_block(pe, U, 1, n, i, xh, xl, kb, dst, N, kb, w, start=False)

        def done(eng, U, n, i):
            eng.wait_ge(block_done, 2 * (U + n * i) + 2)

        def evac(dve, U, n, i, dst, N=T, lo_p=0, hi_p=P, last=True):
            ins = dve.tensor_tensor(dst, psU[U % 2][lo_p:hi_p, 0:N], RS[lo_p:hi_p, 0:N], ALU.mult)
            if last:
                ins.then_inc(evacuated, 1)
            return ins

        c_x, c_hi, c_lo = sem("x_turned"), sem("x_hi"), sem("x_lo")
        c_sq, c_acc = sem("x_sq"), sem("x_acc")
        s_nrm, s_rs = sem("x_ms"), sem("x_rms")

        def apart(eng):
            eng.nop(nofuse=True)

        def act_chunk(act, c, kc, v, xh, N):
            apart(act)
            act.activation(ch(xh, kc, N), ch(X, kc, N), ACT.Copy,
                           scale=VA[:, bass.ds(v + kc, 1)]).then_inc(c_hi, 1)

        def act_square(act, c, par, kc, N, wait=True):
            if wait:
                act.wait_ge(c_acc, c - 1)
            apart(act)
            act.activation(SQ[:, par, 0:N], ch(X, kc, N), ACT.Square).then_inc(c_sq, 1)

        def dve_chunk(dve, c, kc, v, xh, xl, N):
            dve.wait_ge(c_hi, c + 1)
            dve.scalar_tensor_tensor(out=ch(xl, kc, N), in0=ch(X, kc, N),
                                     scalar=VA[:, bass.ds(v + kc, 1)], in1=ch(xh, kc, N),
                                     op0=ALU.mult, op1=ALU.subtract).then_inc(c_lo, 1)

        def pool_square(pool, c, par, N, first=False):
            pool.wait_ge(c_sq, c + 1)
            if first:
                pool.tensor_copy(ACC[:, 0:N], SQ[:, par, 0:N]).then_inc(c_acc, 1)
            else:
                pool.wait_ge(c_acc, c)
                pool.tensor_tensor(ACC[:, 0:N], ACC[:, 0:N], SQ[:, par, 0:N], ALU.add)\
                    .then_inc(c_acc, 1)

        def pe_norm(pe, k, N):
            pe.wait_ge(c_acc, 16 * k + 16)
            pe.matmul(psN[:, 0:N], i2048, ACC[:, 0:N], start=True, stop=True).then_inc(s_nrm, 1)

        def invert_rms(act, pairs, then, n, scale=1.0, whole=None):
            for dst, src in pairs:
                ins = act.activation(dst, src, ACT.Ln, bias=con[:, K_EPS:K_EPS + 1], scale=scale)
            ins.then_inc(then, 1)
            act.wait_ge(then, 2 * n + 1)
            whole = dst if whole is None else whole
            act.activation(whole, whole, ACT.Exp, scale=-0.5).then_inc(then, 1)

        def root_rms(act, dst, src, then, n):
            act.activation(dst, src, ACT.Sqrt, bias=con[:, K_EPS:K_EPS + 1]).then_inc(then, 1)

        def invert_root(dve, buf, then, n):
            dve.wait_ge(then, 2 * n + 1)
            dve.reciprocal(buf, buf).then_inc(then, 1)
            dve.wait_ge(then, 2 * n + 2)

        def dve_norm(dve, k, N):
            dve.wait_ge(s_rs, 2 * k + 2)

        def act_norm(act, k, N):
            act.wait_ge(s_nrm, k + 1)
            invert_rms(act, [(RS[:, 0:N], psN[:, 0:N])], s_rs, k)

        s_con, s_va, s_vb, s_x = sem("con_in"), sem("va_in"), sem("vb_in"), sem("x_in")
        s_vbz, s_vt, s_v = sem("vb_zero"), sem("vec_turned"), sem("vec_ready")
        s_xt, s_fb = sem("x_chunk_turned"), sem("fbias_in")
        ng_t, ng_c, ng_s = sem("ng_turned"), sem("ng_copied"), sem("ng_sigmoid")
        xtok = G[:, 0:4096].rearrange("p (t d) -> p t d", t=2)
        mtok = G[0:META, 4096:6144]
        va_in, vb_in = G[:, 6144:6272], G[:, 6272:6400]
        x_banks = [psS[0], psS[1], psT[1], psO]

        fbias = sb("f_bias", [FOX_H, 1])
        c_row = W[0:FOX_H, 3600:4112].rearrange("p (a n) -> p a n", a=2)
        gtok = sb("nsa_gates_tok", [P, 2, 24])
        gtr = sb("nsa_gates", [P, NSA_H, 6])
        w2k = G[:, 8000:8384].rearrange("p (h d) -> p h d", h=2)
        w2v = G[:, 8384:8640].rearrange("p (h d) -> p h d", h=2)

        qr, kr, vr = W[:, 0:256], W[:, 256:512], W[:, 512:768]
        fsq = W[:, 768:1280].rearrange("p (a n) -> p a n", a=2)
        fq, fk = W[:, 1280:1536], W[:, 1536:1792]
        fv = W[:, 1792:2048].rearrange("p (t d) -> p t d", t=2)
        fs, fpt = W[:, 2048:2432], W[:, 2432:2816]
        fcm = W[0:FOX_H, 3072:3584].rearrange("p (a n) -> p a n", a=2)
        fsm = W[:, 3584:3592]
        fz = W[0:24, 4112:4880].rearrange("p (a n) -> p a n", a=3)

        fx_z, fx_za, x_final = sem("fx_logit"), sem("fx_logsig"), sem("x_final")
        fx_sq, fx_ssq, fx_nrm, fx_qk = (sem("fx_" + n) for n in ("sq", "ssq", "nrm", "qk"))
        fx_cm, fx_s, fx_ttr, fx_e, fx_p = (sem("fx_" + n) for n in ("cm", "s", "ttr", "e", "p"))
        fx_t, fx_pt, fx_o, fx_ohi, fx_olo = (sem("fx_" + n) for n in ("t", "pt", "o", "ohi", "olo"))
        fx_vt, fx_v = sem("fx_vt"), sem("fx_v")
        ch_start, ch_fox = sem("dve_start"), sem("dve_fox")

        def fox_scores(pe, h):
            pe.wait_ge(fx_qk, 2 * h + 2)
            pe.wait_ge(fx_cm, h + 1)
            for q0, cols, nk in ((P, slice(0, T), T), (0, slice(T, T + P), P)):
                dst = psS[0][:, cols]
                pe.matmul(dst, fq[:, q0:q0 + P], fk[:, 0:nk], start=True, stop=False)
                pe.matmul(dst, ones[0:FOX_H, 0:P], fcm[:, 0, 0:nk], start=False, stop=False)
                mm = pe.matmul(dst, fcm[:, 1, q0:q0 + P], ones[0:FOX_H, 0:nk], start=False, stop=True)
            mm.then_inc(fx_s, 1)

        def fox_turn(pe, h):
            pe.wait_ge(fx_p, h + 1)
            pe.transpose(psT[0][:, 0:P], fs[:, T:T + P], ident)
            pe.transpose(psT[0][:, P:T], fs[:, 0:P], ident)
            pe.transpose(psT[0][:, T:T + P], fs[:, P:T], ident).then_inc(fx_t, 1)

        def fox_values(pe, h):
            pe.wait_ge(fx_pt, h + 1)
            pe.wait_ge(fx_v, h + 1)
            pe.matmul(psO[:, 0:T], fv[:, 0, :], fpt[:, 0:T], start=True, stop=False)
            pe.matmul(psO[:, P:T], fv[:, 1, :], fpt[:, T:T + P], start=False, stop=True)\
              .then_inc(fx_o, 1)

        def fox_ssq(pe, h, first=False):
            pe.wait_ge(fx_sq, 2 * h + 2)
            if not first:
                pe.wait_ge(fx_nrm, 2 * h)
            pe.matmul(psN[:, :], i128, fsq.rearrange("p a n -> p (a n)"), start=True, stop=True)\
              .then_inc(fx_ssq, 1)

        def fox_root(act, h):
            act.wait_ge(fx_ssq, h + 1)
            root_rms(act, fsq.rearrange("p a n -> p (a n)"), psN[:, :], fx_nrm, h)

        def fox_softmax(dve, ch, h):
            dve.wait_ge(fx_s, h + 1)
            apart(dve)
            dve.tensor_tensor_reduce(fs[:, 0:T], psS[0][:, 0:T], tri, 1.0, 3 * BIG, ALU.add,
                                     ALU.min, fsm[:, 0:1])
            dve.tensor_tensor_reduce(fs[:, T:T + P], psS[0][:, T:T + P], tri[:, P:T], 1.0, 3 * BIG,
                                     ALU.add, ALU.min, fsm[:, 1:2]).then_inc(fx_ttr, 1)

        def fox_exp(act, h):
            act.wait_ge(fx_ttr, h + 1)
            act.activation(fs[:, 0:T], fs[:, 0:T], ACT.Exp, bias=fsm[:, 0:1], scale=-1.0,
                           accum_out=fsm[:, 2:3])
            act.activation(fs[:, T:T + P], fs[:, T:T + P], ACT.Exp, bias=fsm[:, 1:2], scale=-1.0,
                           accum_out=fsm[:, 3:4]).then_inc(fx_e, 1)

        def fox_weights(dve, ch, h):
            dve.wait_ge(fx_e, h + 1)
            ch.link(dve.reciprocal(fsm[:, 4:6], fsm[:, 2:4]))
            dve.tensor_scalar(fs[:, 0:T], fs[:, 0:T], fsm[:, 4:5], None, ALU.mult)
            dve.tensor_scalar(fs[:, T:T + P], fs[:, T:T + P], fsm[:, 5:6], None, ALU.mult)\
               .then_inc(fx_p, 1)

        def fox_normed(dve, h):
            invert_root(dve, fsq.rearrange("p a n -> p (a n)"), fx_nrm, h)
            for which, (src, dst, v) in enumerate(((qr, fq, V_FQ), (kr, fk, V_FK))):
                dve.scalar_tensor_tensor(out=dst, in0=src, scalar=VA[:, v:v + 1],
                                         in1=fsq[:, which, :], op0=ALU.mult, op1=ALU.mult)\
                   .then_inc(fx_qk, 1)

        def fox_square(act, h, U, n, which, src):
            act.wait_ge(evacuated, U + n * h + 1)
            act.activation(fsq[:, which, :], src, ACT.Square).then_inc(fx_sq, 1)

        def fox_copy_pt(act, h):
            act.wait_ge(fx_t, h + 1)
            act.activation(fpt, psT[0][:, 0:T + P], ACT.Copy).then_inc(fx_pt, 1)

        def fox_out_hi(act, h):
            act.wait_ge(fx_o, h + 1)
            act.activation(BH[:, h, 0:T], psO[:, 0:T], ACT.Copy).then_inc(fx_ohi, 1)

        def fox_out_lo(dve, h):
            dve.wait_ge(fx_ohi, h + 1)
            dve.tensor_tensor(BL[:, h, 0:T], psO[:, 0:T], BH[:, h, 0:T], ALU.subtract)\
               .then_inc(fx_olo, 1)

        def fox_decay(dve, h):
            for s in range(2):
                ins = dve.tensor_scalar(fcm[:, s, :], c_row[:, s, :], con[0:FOX_H, bass.ds(K_ID + h, 1)], None,
                                        ALU.mult)
            ins.then_inc(fx_cm, 1)

        def area(lo_c, n, p=P, a=2):
            return W[0:p, lo_c:lo_c + n].rearrange("p (a n) -> p a n", a=a)

        ksm, kwm, kst, kwt = area(3600, 512), area(4112, 512), area(4624, 512, 64), area(5136, 512, 64)
        vs_t = W[:, 5648:6160].rearrange("p (g t d) -> p g t d", g=2, t=2)
        vw_t = W[:, 6160:6672].rearrange("p (g t d) -> p g t d", g=2, t=2)
        kcm, kct = W[:, 6672:6702], W[0:64, 6702:6732]
        vc_t = W[0:NB_C, 6732:6988].rearrange("p (g d) -> p g d", g=2)
        kraw, ktraw, vraw = area(0, 512), area(512, 512, 64), area(1280, 512)
        ksq, ktsq = W[:, 1792:2304], W[0:64, 2304:2816]
        w1s = G[:, 2048:5120].rearrange("p (s j n) -> p s j n", s=3, j=4)
        cpk = G[:, 5120:6080].rearrange("p (j n) -> p j n", j=32)
        cpt = G[0:64, 6080:7040].rearrange("p (j n) -> p j n", j=32)
        cpv = G[:, 7040:8000].rearrange("p (j n) -> p j n", j=32)
        hsl = W[:, 2816:2936].rearrange("p (v h n) -> p v h n", v=2, h=2)
        kcr, kctr = W[:, 2936:2966], W[0:64, 2966:2996]
        kcs, kcts = W[:, 2996:3026], W[0:64, 3026:3056]
        kcrs = W[:, 3056:3086]

        nk_sq, nk_ssq, nk_nrm, nk_k = (sem("nk_" + n) for n in ("sq", "ssq", "nrm", "k"))
        nk_vt, nk_v = sem("nk_vt"), sem("nk_v")
        cw_full = [sem(f"cw_full{n}") for n in range(3)]
        cw_used, cp_ready = sem("cw_used"), sem("cp_ready")
        cm_hs, cm_kc, cm_kcr, cm_sq, cm_ms, cm_rs = (
            sem("cm_" + n) for n in ("hs", "kc", "kcr", "sq", "ms", "rs"))
        w2_full = sem("w2_full")

        CPIECES = [(src, j) for src in range(3) for j in range(0, 32, 4)]
        w1k = a["cmp_w1_k"][0].rearrange("(j d) n -> d j n", d=NSA_DK)
        w1v = a["cmp_w1_v"][0].rearrange("(j d) n -> d j n", d=NSA_DV)
        cmp_banks = [psS[0], psS[1], psT[0], psO]

        def cmp_load(pool, m):
            src, j = CPIECES[m]
            if m >= 3:
                pool.wait_ge(cw_used, m - 2)
            if src == 0:
                pool.dma_start(w1s[:, m % 3], w1k[0:P, j:j + 4]).then_inc(cw_full[m % 3], 16)
            elif src == 1:
                pool.dma_start(w1s[0:64, m % 3], w1k[P:NSA_DK, j:j + 4]).then_inc(cw_full[m % 3], 16)
            else:
                pool.dma_start(w1s[:, m % 3], w1v[:, j:j + 4]).then_inc(cw_full[m % 3], 16)

        def cmp_windows(pool, src_ap, pe_col, p, dst):
            for g in range(NSA_G):
                for half in range(2):
                    j0 = 16 * half
                    win = src_ap[0:p, g, j0:j0 + 240].rearrange("p (n j) -> p j n", j=16)
                    pe_b = VB[0:p, pe_col + j0:pe_col + j0 + 16].unsqueeze(2)\
                        .broadcast_to([p, 16, NB_C])
                    ins = pool.tensor_tensor(dst[0:p, j0:j0 + 16, g * NB_C:(g + 1) * NB_C], win, pe_b,
                                             ALU.add)
            ins.then_inc(cp_ready, 1)

        def cmp_piece(pe, m):
            src, j = CPIECES[m]
            pe.wait_ge(cw_full[m % 3], 16 * (m // 3 + 1))
            pe.wait_ge(cp_ready, src + 1)
            p = 64 if src == 1 else P
            x = (cpk, cpt, cpv)[src]
            for jj in range(4):
                for h in range(2):
                    mm = pe.matmul(cmp_banks[2 * (src == 2) + h][:, 0:30],
                                   w1s[0:p, m % 3, jj, h * P:(h + 1) * P], x[0:p, j + jj, :],
                                   start=(j + jj == 0 and src != 1),
                                   stop=(j + jj == 31 and src != 0))
            mm.then_inc(cw_used, 1)

        def nsa_turn_v(pe, n, U):
            pe.wait_ge(evacuated, U + 1)
            if n:
                pe.wait_ge(nk_v, n)
            for t in range(2):
                mm = pe.transpose(psT[1][:, t * P:(t + 1) * P], vraw[:, n % 2, t * P:(t + 1) * P], ident)
            mm.then_inc(nk_vt, 1)

        qt_sq = W[0:64, 1536:2048]
        qmr, qtr, qm, qt = area(0, 512), area(512, 512, 64), area(1024, 512), area(1536, 512, 64)
        nsq = W[:, 2048:2560]
        nsm = W[:, 2560:2592]
        ncs = W[:, 2592:2622].rearrange("p (t n) -> p t n", t=2)
        ntab, nsp = G[:, 4096:4352], G[:, 4352:5120].rearrange("p (b n) -> p b n", b=2)
        npt = G[:, 5120:5888].rearrange("p (b n) -> p b n", b=2)
        nptc = G[0:NB_C, 5888:6144]
        vs_c = G[:, 6144:6400].rearrange("p (t d) -> p t d", t=2)
        vw_c = G[:, 6400:6656].rearrange("p (t d) -> p t d", t=2)
        vc_c = G[0:NB_C, 6656:6784]
        nq_sq, nq_ssq, nq_nrm, nq_q = (sem("nq_" + n) for n in ("sq", "ssq", "nrm", "q"))
        na_s, na_ttr, na_e, na_p, na_t = (sem("na_" + n) for n in ("s", "ttr", "e", "p", "t"))
        na_pta, na_ptd, na_o, na_ohi, na_olo, na_vc = (
            sem("na_" + n) for n in ("pta", "ptd", "o", "ohi", "olo", "vcur"))
        ch_nq = [sem("dve_nq_a"), sem("dve_nq_b")]

        def nsa_scores(pe, n, g, a_):
            if a_:
                pe.wait_ge(na_ttr, n)
            for br, (km, kt) in enumerate(((ksm, kst), (kwm, kwt))):
                for q0, cols, nk in ((P, slice(0, T), T), (0, slice(T, T + P), P)):
                    dst = psS[br][:, cols]
                    pe.matmul(dst, qm[:, a_, q0:q0 + P], km[:, g, 0:nk], start=True, stop=False)
                    mm = pe.matmul(dst, qt[:, a_, q0:q0 + P], kt[:, g, 0:nk], start=False, stop=True)
            kcg, kctg = (k.rearrange("p (g n) -> p g n", g=2) for k in (kcm, kct))
            for t in range(2):
                dst = psS[0][:, 384 + 16 * t:384 + 16 * t + NB_C]
                pe.matmul(dst, qm[:, a_, t * P:(t + 1) * P], kcg[:, g, :], start=True, stop=False)
                mm = pe.matmul(dst, qt[:, a_, t * P:(t + 1) * P], kctg[:, g, :], start=False, stop=True)
            mm.then_inc(na_s, 1)

        def nsa_turn(pe, n):
            pe.wait_ge(na_p, n + 1)
            for br in range(2):
                pe.transpose(psT[br][:, 0:P], nsp[:, br, T:T + P], ident)
                pe.transpose(psT[br][:, P:T], nsp[:, br, 0:P], ident)
                pe.transpose(psT[br][:, T:T + P], nsp[:, br, P:T], ident)
                mm = pe.transpose(psT[br][0:NB_C, 384:512], ncs[:, br, :], ident)
            mm.then_inc(na_t, 1)

        def nsa_values(pe, n, a_):
            pe.wait_ge(na_pta, n + 1)
            pe.wait_ge(na_ptd, n + 1)
            if a_:
                pe.wait_ge(na_olo, n)
            o = psO[:, 0:T]
            pe.matmul(o, vs_c[:, 0, :], npt[:, 0, 0:T], start=True, stop=False)
            pe.matmul(o, vw_c[:, 0, :], npt[:, 1, 0:T], start=False, stop=False)
            pe.matmul(o, vc_c[:, :], nptc, start=False, stop=False)
            pe.matmul(psO[:, P:T], vs_c[:, 1, :], npt[:, 0, T:T + P], start=False, stop=False)
            pe.matmul(psO[:, P:T], vw_c[:, 1, :], npt[:, 1, T:T + P], start=False, stop=True)\
              .then_inc(na_o, 1)

        def nsa_softmax(dve, ch, n):
            ch.link(dve.tensor_scalar(ntab, con[:, K_DIST:K_DIST + T],
                                      con[:, bass.ds(K_SLOPE + n, 1)], None, ALU.mult))
            dve.wait_ge(na_s, n + 1)
            apart(dve)
            for br in range(2):
                dve.tensor_tensor_reduce(nsp[:, br, 0:T], psS[br][:, 0:T], ntab, 1.0, 3 * BIG,
                                         ALU.add, ALU.min, nsm[:, 2 * br + 1:2 * br + 2])
                dve.tensor_tensor_reduce(nsp[:, br, T:T + P], psS[br][:, T:T + P], ntab[:, P:T], 1.0,
                                         3 * BIG, ALU.add, ALU.min, nsm[:, 2 * br:2 * br + 1])
            distc = con[:, K_DISTC:K_DISTC + 30].rearrange("p (t n) -> p t n", t=2)
            psc = psS[0][:, 384:416].rearrange("p (t n) -> p t n", t=2)[:, :, 0:NB_C]
            ch.link(dve.scalar_tensor_tensor(out=ncs, in0=distc, scalar=con[:, bass.ds(K_SLOPE + n, 1)],
                                             in1=psc, op0=ALU.mult, op1=ALU.add))
            ch.link(dve.tensor_reduce(nsm[:, 4:6], ncs, AX, ALU.min))
            dve.tensor_tensor(ncs, ncs, nsm[:, 4:6].unsqueeze(2).broadcast_to([P, 2, NB_C]),
                              ALU.subtract).then_inc(na_ttr, 1)

        def nsa_exp(act, n):
            act.wait_ge(na_ttr, n + 1)
            for br in range(2):
                act.activation(nsp[:, br, 0:T], nsp[:, br, 0:T], ACT.Exp,
                               bias=nsm[:, 2 * br + 1:2 * br + 2], scale=-1.0,
                               accum_out=nsm[:, 6 + 2 * br + 1:6 + 2 * br + 2])
                act.activation(nsp[:, br, T:T + P], nsp[:, br, T:T + P], ACT.Exp,
                               bias=nsm[:, 2 * br:2 * br + 1], scale=-1.0,
                               accum_out=nsm[:, 6 + 2 * br:6 + 2 * br + 1])
            act.activation(ncs, ncs, ACT.Exp, scale=-1.0).then_inc(na_e, 1)

        def nsa_weights(dve, ch, n):
            dve.wait_ge(na_e, n + 1)
            maskc = con[:, K_MASKC:K_MASKC + 30].rearrange("p (t n) -> p t n", t=2)
            ch.link(dve.tensor_tensor(ncs, ncs, maskc, ALU.mult))
            ch.link(dve.tensor_reduce(nsm[:, 10:12], ncs, AX, ALU.add))
            ch.link(dve.tensor_scalar(nsm[:, 12:18], nsm[:, 6:12], 1e-30, None, ALU.max))
            ch.link(dve.reciprocal(nsm[:, 18:24], nsm[:, 12:18]))
            ch.link(dve.tensor_tensor(nsm[:, 24:30], nsm[:, 18:24],
                                      gtr[:, bass.ds(n, 1), :].rearrange("p a b -> p (a b)"), ALU.mult))
            for br in range(2):
                dve.tensor_scalar(nsp[:, br, 0:T], nsp[:, br, 0:T],
                                  nsm[:, 24 + 2 * br + 1:24 + 2 * br + 2], None, ALU.mult)
                dve.tensor_scalar(nsp[:, br, T:T + P], nsp[:, br, T:T + P],
                                  nsm[:, 24 + 2 * br:24 + 2 * br + 1], None, ALU.mult)
            dve.tensor_tensor(ncs, ncs, nsm[:, 28:30].unsqueeze(2).broadcast_to([P, 2, NB_C]),
                              ALU.mult).then_inc(na_p, 1)

        def nsa_copy_a(act, n):
            act.wait_ge(na_t, n + 1)
            act.activation(npt[:, 0, :], psT[0][:, 0:384], ACT.Copy)
            act.activation(nptc[:, 0:P], psT[0][0:NB_C, 384:512], ACT.Copy).then_inc(na_pta, 1)

        def nsa_copy_d(dve, n):
            dve.wait_ge(na_t, n + 1)
            dve.tensor_copy(npt[:, 1, :], psT[1][:, 0:384])
            dve.tensor_copy(nptc[:, P:T], psT[1][0:NB_C, 384:512]).then_inc(na_ptd, 1)

        def nsa_copy_v(act, n):
            act.wait_ge(nk_vt, n + 1)
            act.activation((vs_t, vw_t)[n // 2][:, n % 2],
                           psT[1][:, 0:T].rearrange("p (t d) -> p t d", t=2), ACT.Copy).then_inc(nk_v, 1)

        def nsa_out_hi(act, n):
            act.wait_ge(na_o, n + 1)
            apart(act)
            act.activation(BH[:, bass.ds(8 + n, 1), 0:T].rearrange("p a n -> p (a n)"), psO[:, 0:T],
                           ACT.Copy).then_inc(na_ohi, 1)

        def nsa_out_lo(dve, n):
            dve.wait_ge(na_ohi, n + 1)
            dve.tensor_tensor(BL[:, bass.ds(8 + n, 1), 0:T].rearrange("p a n -> p (a n)"),
                              psO[:, 0:T],
                              BH[:, bass.ds(8 + n, 1), 0:T].rearrange("p a n -> p (a n)"),
                              ALU.subtract).then_inc(na_olo, 1)

        PASSES = ((0, 16), (16, 16), (32, 12))
        u_ffn, u = [], U_FFN
        for _, n_h in PASSES:
            u_ffn.append((u, u + 2 * n_h))
            u += 2 * n_h + KC
        U_END1 = u
        gsl = W[:, 0:512].rearrange("p (a n) -> p a n", a=2)
        hup, hpr = W[:, 512:768], W[:, 768:1024]
        ff_silu, ff_h, ff_hi, ff_lo = (sem("ff_" + n) for n in ("silu", "h", "hi", "lo"))
        up_t = W[:, 0:512].rearrange("p (a n) -> p a n", a=2)
        up_m = W[:, 512:768]
        up_sg, up_mr, up_hi, up_lo = (sem("up_" + n) for n in ("sg", "m", "hi", "lo"))

        w_upf = a["w_up_fox"][0].rearrange("(k p) n -> p k n", p=P)
        w_upn = a["w_up_nsa"][0].rearrange("(k p) n -> p k n", p=P)
        w_o1 = a["w_out"][0].rearrange("(k p) n -> p k n", p=P)
        w_fg = a["w_ffn_gate"][0].rearrange("(k p) n -> p k n", p=P)
        w_fu = a["w_ffn_up"][0].rearrange("(k p) n -> p k n", p=P)
        w_fd = a["w_ffn_down"][0].rearrange("(k p) n -> p k n", p=P)

        s_out = [sem("out0"), sem("out1")]
        o_t, o_c = sem("out_turned"), sem("out_copied")
        otok = G[:, 4352:8448].rearrange("p (t d) -> p t d", t=2)

        U_AG = U_END1
        U_AT = U_AG + KC
        U_AO = U_AT + 4 * GQ_KV
        U_GG = U_AO + KC
        U_LR = U_GG + KC
        U_GL = U_LR + 1
        U_GO = U_GL + 8 * GLA_H
        U_END = U_GO + KC
        w_ai = a["attn_w_in_2"][0].rearrange("(k p) n -> p k n", p=P)
        w_ao = a["attn_w_out_2"][0].rearrange("(k p) n -> p k n", p=P)
        w_gi = a["gla_w_in_2"][0].rearrange("(k p) n -> p k n", p=P)
        w_go = a["gla_w_out_2"][0].rearrange("(k p) n -> p k n", p=P)

        con2 = W[:, 6200:6200 + N_K2]
        cos, sin = con2[:, 0:T], con2[:, T:2 * T]
        swap, upto, after = (con2[:, 2 * T + P * n:2 * T + P * (n + 1)] for n in range(3))

        def wide(c, n, N=TM):
            return W[:, c:c + n * N].rearrange("p (a n) -> p a n", n=N)

        aw, avr = wide(0, 3), W[:, 816:1088]
        asq, axn, aqk = wide(1088, 3), wide(1904, 3), wide(2720, 3)
        arot = wide(3536, 3, T)
        ap_ = wide(4304, 5)
        asm = W[:, 5664:5679]
        amq = W[:, 6084:6116]
        avt = W[:, 5700:6084].rearrange("p (t d) -> p t d", t=3)
        apt = G[:, 4352:5984].rearrange("p (k h n) -> p k h n", k=3, h=2)
        apr = G[:, 5984:6528].rearrange("p (h n) -> p h n", h=2)
        ga_sg, aq_sq, aq_ssq, aq_root, aq_n, aq_perm, aq_r = (
            sem("ga_" + n) for n in ("gate", "sq", "ssq", "root", "n", "perm", "rope"))
        aq_vt, aq_v, aq_s, aq_min, aq_e, aq_p, aq_t, aq_pa, aq_pd, aq_o, aq_pr, aq_hi, aq_lo = (
            sem("ga_" + n) for n in ("vt", "v", "s", "min", "e", "p", "t", "pa", "pd", "o", "pr",
                                     "hi", "lo"))
        ch_second = sem("dve_second")
        O_GA, O_GL = 0, 2 * GQ_KV
        s_banks = [psS[0], psS[1], psT[0], psT[1], psN]

        def ga_ssq(pe, j, first=False):
            pe.wait_ge(aq_sq, j + 1)
            if not first:
                pe.wait_ge(aq_pa, j)
                pe.wait_ge(aq_pd, j)
            for n, b in enumerate((psT[0], psS[0], psS[1])):
                mm = pe.matmul(b[:, 0:TM], i128, asq[:, n], start=True, stop=True)
            mm.then_inc(aq_ssq, 1)

        def ga_perm(pe, j, first=False):
            pe.wait_ge(aq_n, j + 1)
            if not first:
                pe.wait_ge(aq_pr, j)
            for n, b in enumerate((psT[0], psT[1], psN)):
                mm = pe.matmul(b[:, 0:T], swap, axn[:, n, 0:T], start=True, stop=True)
            mm.then_inc(aq_perm, 1)
            for t in range(2):
                pe.transpose(psO[:, t * P:(t + 1) * P], avr[:, t * P:(t + 1) * P], ident)
            pe.transpose(psO[0:META, T:T + P], avr[:, T:TM], ident).then_inc(aq_vt, 1)

        def ga_scores(pe, j):
            pe.wait_ge(aq_r, j + 1)
            for h in range(2):
                for t in range(2):
                    pe.matmul(s_banks[2 * h + t][:, 0:TM], aqk[:, 1 + h, t * P:(t + 1) * P],
                              aqk[:, 0, :], start=True, stop=True)
            pe.matmul(psN[0:2 * META, 0:TM], amq, aqk[:, 0, :], start=True, stop=True)\
              .then_inc(aq_s, 1)

        def ga_turn(pe, j):
            pe.wait_ge(aq_p, j + 1)
            for n in range(5):
                p = P if n < 4 else 2 * META
                for k in range(3):
                    kp = P if k < 2 else META
                    mm = pe.transpose(s_banks[n][0:kp, k * p:(k + 1) * p],
                                      ap_[0:p, n, k * P:k * P + kp], ident[0:p, 0:p])
            mm.then_inc(aq_t, 1)

        def ga_values(pe, j):
            pe.wait_ge(aq_pa, j + 1)
            pe.wait_ge(aq_pd, j + 1)
            pe.wait_ge(aq_v, j + 1)
            for h, b in enumerate((psO, psN)):
                for k in range(3):
                    kp = P if k < 2 else META
                    mm = pe.matmul(b[:, 0:TM], avt[0:kp, k], apt[0:kp, k, h, :], start=k == 0,
                                   stop=k == 2)
            mm.then_inc(aq_o, 1)

        def ga_normed(dve, c, j):
            dve.wait_ge(aq_root, 2 * j + 2)
            dve.scalar_tensor_tensor(out=axn[:, 0], in0=aw[:, 0], scalar=VA[:, V_AK:V_AK + 1],
                                     in1=asq[:, 0], op0=ALU.mult, op1=ALU.mult)
            dve.scalar_tensor_tensor(out=axn[:, 1:3], in0=aw[:, 1:3], scalar=VA[:, V_AQ:V_AQ + 1],
                                     in1=asq[:, 1:3], op0=ALU.mult, op1=ALU.mult).then_inc(aq_n, 1)
            dve.wait_ge(aq_n, j + 1)

        def ga_rope(dve, c, j):
            dve.wait_ge(aq_perm, j + 1)
            for n, b in enumerate((psT[0], psT[1], psN)):
                dve.tensor_tensor(arot[:, n], b[:, 0:T], sin, ALU.mult)
            dve.tensor_copy(aqk[:, 0, T:TM], axn[:, 0, T:TM])
            dve.tensor_copy(amq.rearrange("p (h n) -> p h n", h=2), axn[:, 1:3, T:TM])
            c.link(dve.tensor_tensor(aqk[:, :, 0:T], axn[:, :, 0:T],
                                     cos.unsqueeze(1).broadcast_to([P, 3, T]), ALU.mult))
            dve.tensor_tensor(aqk[:, :, 0:T], aqk[:, :, 0:T], arot, ALU.add).then_inc(aq_r, 1)

        def ga_min(dve, j):
            dve.wait_ge(aq_s, j + 1)
            for n in range(5):
                p = P if n < 4 else 2 * META
                ins = dve.tensor_reduce(asm[0:p, n:n + 1], s_banks[n][0:p, 0:TM], AX, ALU.min)
            ins.then_inc(aq_min, 1)

        def ga_exp(act, j):
            act.wait_ge(aq_min, j + 1)
            for n in range(5):
                p = P if n < 4 else 2 * META
                ins = act.activation(ap_[0:p, n], s_banks[n][0:p, 0:TM], ACT.Exp,
                                     bias=asm[0:p, n:n + 1], scale=-1.0,
                                     accum_out=asm[0:p, 5 + n:6 + n])
            ins.then_inc(aq_e, 1)

        def ga_weights(dve, c, j):
            dve.wait_ge(aq_e, j + 1)
            dve.reciprocal(asm[:, 10:14], asm[:, 5:9])
            c.link(dve.reciprocal(asm[0:2 * META, 14:15], asm[0:2 * META, 9:10]))
            for n in range(5):
                p = P if n < 4 else 2 * META
                ins = dve.tensor_scalar(ap_[0:p, n], ap_[0:p, n], asm[0:p, 10 + n:11 + n], None,
                                        ALU.mult)
            ins.then_inc(aq_p, 1)

        def ga_copy_pt(copy, n):
            h, t = divmod(n, 2)
            copy(apt[:, 0:2, h, t * P:(t + 1) * P],
                 s_banks[n][:, 0:2 * P].rearrange("p (k n) -> p k n", k=2))
            return copy(apt[0:META, 2, h, t * P:(t + 1) * P], s_banks[n][0:META, 2 * P:3 * P])

        def act_copy(act):
            return lambda dst, src: act.activation(dst, src, ACT.Copy)

        def ga_copy_a(act, j):
            act.wait_ge(aq_t, j + 1)
            for n in range(2):
                ins = ga_copy_pt(act_copy(act), n)
            ins.then_inc(aq_pa, 1)

        def ga_copy_d(dve, j):
            dve.wait_ge(aq_t, j + 1)
            for n in range(2, 4):
                ga_copy_pt(dve.tensor_copy, n)
            dve.tensor_copy(apt[:, 0:2, :, T:TM],
                            psN[:, 0:4 * META].rearrange("p (k h n) -> p k h n", k=2, h=2))
            dve.tensor_copy(apt[0:META, 2, :, T:TM],
                            psN[0:META, 4 * META:6 * META].rearrange("p (h n) -> p h n", h=2))\
               .then_inc(aq_pd, 1)

        def ga_copy_v(act, j):
            act.wait_ge(aq_vt, j + 1)
            act.activation(avt[:, 0:2], psO[:, 0:T].rearrange("p (t d) -> p t d", t=2), ACT.Copy)
            act.activation(avt[0:META, 2], psO[0:META, T:T + P], ACT.Copy).then_inc(aq_v, 1)

        def ga_square(act, j):
            act.activation(asq, aw, ACT.Square).then_inc(aq_sq, 1)

        def ga_root(act, j):
            act.wait_ge(aq_ssq, j + 1)
            invert_rms(act, [(asq[:, n], b[:, 0:TM]) for n, b in enumerate((psT[0], psS[0], psS[1]))],
                       aq_root, j, whole=asq)

        def ga_gated(dve, j):
            if not isinstance(j, int) or j:
                dve.wait_ge(aq_lo, j)
            dve.wait_ge(aq_o, j + 1)
            for h, b in enumerate((psO, psN)):
                ins = dve.tensor_tensor(apr[:, h], b[:, 0:TM], G[:, bass.ds(2 * TM * j + TM * h, TM)],
                                        ALU.mult)
            ins.then_inc(aq_pr, 1)

        def ga_split(pool, j):
            pool.wait_ge(aq_pr, j + 1)
            apart(pool)
            pool.tensor_copy(AH[:, bass.ds(2 * j, 2), :], apr).then_inc(aq_hi, 1)
            pool.wait_ge(aq_hi, j + 1)
            apart(pool)
            pool.tensor_tensor(AL[:, bass.ds(2 * j, 2), :], apr, AH[:, bass.ds(2 * j, 2), :],
                               ALU.subtract).then_inc(aq_lo, 1)

        GC = T // GLA_C
        lqk, lvr = wide(0, 4), wide(1088, 2)
        lcum = W[:, 1632:2660].rearrange("p (s c n) -> p s c n", s=2, c=2)
        lcm = W[:, 2660:2692].rearrange("p (c n) -> p c n", c=2)
        lz, ll = wide(2724, 4), wide(3812, 4)
        lA = W[:, 2724:3492].rearrange("p (t n) -> p t n", t=3)
        lBm = W[:, 3492:3748].rearrange("p (t n) -> p t n", t=2)
        lsq = wide(2724, 4, T)
        lo_o = wide(3812, 4, T)
        lqd = W[:, 3812:4836].rearrange("p (s c n) -> p s c n", s=2, c=2)
        lvt = W[:, 4900:5924].rearrange("p (t d) -> p t d", t=2)
        lvm = W[0:META, 5924:6436]
        lr = W[0:32, 6436:6708]
        lgk = W[0:32, 7120:7632].rearrange("p (s d) -> p s d", s=2)
        lrs = W[:, 7632:7888]
        lk = G[:, 4352:8448].rearrange("p (s n c t) -> p s n c t", s=2, n=GC, c=2)
        lkm = G[:, 8448:8576].rearrange("p (n c t) -> p n c t", n=GC, c=2)
        lkr = [[(0, (n + 1) * GLA_C) for n in range(GC)], [(n * GLA_C, T) for n in range(GC)]]
        gl_sg, gl_gk, gl_zero, gl_z, gl_zp, gl_l, gl_ex, gl_exp, gl_m = (
            sem("gl_" + n) for n in ("gate", "gk", "zero", "z", "zp", "l", "ex", "exp", "m"))
        gl_s, gl_a, gl_o, gl_sq, gl_ssq, gl_root, gl_on, gl_hi, gl_lo, gl_vt, gl_v = (
            sem("gl_" + n) for n in ("s", "a", "o", "sq", "ssq", "root", "on", "hi", "lo", "vt", "v"))
        z_banks = [psN, psO, psS[0], psS[1]]

        def gl_load(act, h):
            if not (isinstance(h, int) and h == 0):
                act.wait_ge(gl_zp, h)
            up = a["gla_gk_up_2"][0]
            act.dma_start(lgk[0:16, 0], up[0][:, bass.ds(256 * h, 256)]).then_inc(gl_gk, 16)
            act.dma_start(lgk[16:32, 1], up[1][:, bass.ds(256 * h, 256)]).then_inc(gl_gk, 16)

        def gl_scores(pe, h):
            pe.wait_ge(gl_m, h + 1)
            def pair(dst, s, n, t):
                for c in range(2):
                    mm = pe.matmul(dst, lk[:, s, n, c, t * P:(t + 1) * P],
                                   lqd[:, s, c, n * GLA_C:(n + 1) * GLA_C], start=c == 0, stop=c == 1)
                return mm
            for t in range(2):
                for n in range(GC):
                    own = n // 2 == t
                    pair(psS[t][:, n * GLA_C:(n + 1) * GLA_C], 0 if n // 2 >= t else 1, n, t)
                    if own:
                        pair(psS[t][:, T + (n % 2) * GLA_C:T + (n % 2 + 1) * GLA_C], 1, n, t)
            for n in range(GC):
                for c in range(2):
                    mm = pe.matmul(psT[1][0:META, n * GLA_C:(n + 1) * GLA_C], lkm[:, n, c, :],
                                   lqd[:, 0, c, n * GLA_C:(n + 1) * GLA_C], start=c == 0, stop=c == 1)
            mm.then_inc(gl_s, 1)

        def gl_mask(dve, c, h):
            dve.wait_ge(gl_s, h + 1)
            for t in range(2):
                own = slice(t * P, (t + 1) * P)
                oth = slice((1 - t) * P, (2 - t) * P)
                dve.tensor_copy(lA[:, t, oth], psS[t][:, oth])
                dve.tensor_tensor(lA[:, t, own], psS[t][:, own], upto, ALU.mult)
                ins = dve.tensor_tensor(lBm[:, t], psS[t][:, T:T + P], after, ALU.mult)
            c.link(ins)
            for t in range(2):
                own = slice(t * P, (t + 1) * P)
                dve.tensor_tensor(lA[:, t, own], lA[:, t, own], lBm[:, t], ALU.add)
            dve.tensor_copy(lA[0:META, 2, :], psT[1][0:META, 0:T]).then_inc(gl_a, 1)

        def gl_out(pe, h):
            pe.wait_ge(gl_a, h + 1)
            pe.wait_ge(gl_v, 4 * h + 4)
            for e in range(4):
                dst = (psO, psN)[e // 2][:, (e % 2) * T:(e % 2 + 1) * T]
                es = slice(e * P, (e + 1) * P)
                pe.matmul(dst, lvt[:, 0, es], lA[:, 0, :], start=True, stop=False)
                pe.matmul(dst, lvt[:, 1, es], lA[:, 1, :], start=False, stop=False)
                mm = pe.matmul(dst, lvm[:, es], lA[0:META, 2, :], start=False, stop=True)
            mm.then_inc(gl_o, 1)

        def gl_turn(pe, h, m):
            pe.wait_ge(evacuated, U_GL + m + 1 + 8 * h)
            if m >= 1:
                pe.wait_ge(gl_v, 4 * h + m)
            b = psT[0]
            for t in range(2):
                pe.transpose(b[:, t * P:(t + 1) * P], lvr[:, m % 2, t * P:(t + 1) * P], ident)
            pe.transpose(b[0:META, T:T + P], lvr[:, m % 2, T:TM], ident).then_inc(gl_vt, 1)

        def gl_copy_v(act, h, m):
            act.wait_ge(gl_vt, 4 * h + m + 1)
            act.activation(lvt[:, :, m * P:(m + 1) * P],
                           psT[0][:, 0:T].rearrange("p (t d) -> p t d", t=2), ACT.Copy)
            act.activation(lvm[:, m * P:(m + 1) * P], psT[0][0:META, T:T + P], ACT.Copy)\
               .then_inc(gl_v, 1)

        def gl_square(act, h):
            act.wait_ge(gl_o, h + 1)
            act.activation(lsq[:, 0:2], psO[:, :].rearrange("p (e n) -> p e n", e=2), ACT.Square)
            act.activation(lsq[:, 2:4], psN[:, :].rearrange("p (e n) -> p e n", e=2), ACT.Square)\
               .then_inc(gl_sq, 1)

        def gl_ssqs(pe, h):
            pe.wait_ge(gl_sq, h + 1)
            for e in range(4):
                mm = pe.matmul(psS[0][:, 0:T], i2048, lsq[:, e], start=e == 0, stop=e == 3)
            mm.then_inc(gl_ssq, 1)

        def gl_rootf(act, h):
            act.wait_ge(gl_ssq, h + 1)
            invert_rms(act, [(lrs, psS[0][:, 0:T])], gl_root, h, scale=4.0)

        def gl_normed(dve, c, h):
            dve.wait_ge(gl_root, 2 * h + 2)
            for e in range(4):
                src = (psO, psN)[e // 2][:, (e % 2) * T:(e % 2 + 1) * T]
                ins = dve.scalar_tensor_tensor(out=lo_o[:, e], in0=src,
                                               scalar=VA[:, V_ON + e:V_ON + e + 1], in1=lrs,
                                               op0=ALU.mult, op1=ALU.mult)
            c.link(ins)
            gate = G[:, bass.ds(4 * T * h, 4 * T)].rearrange("p (e n) -> p e n", e=4)
            dve.tensor_tensor(lo_o, lo_o, gate, ALU.mult).then_inc(gl_on, 1)

        def gl_out_hi(act, h):
            act.wait_ge(gl_on, h + 1)
            apart(act)
            act.activation(AH[:, bass.ds(4 * h, 4), 0:T], lo_o, ACT.Copy).then_inc(gl_hi, 1)

        def gl_out_lo(dve, h):
            dve.wait_ge(gl_hi, h + 1)
            dve.tensor_tensor(AL[:, bass.ds(4 * h, 4), 0:T], lo_o, AH[:, bass.ds(4 * h, 4), 0:T],
                              ALU.subtract).then_inc(gl_lo, 1)

        def gl_logits(pe, h, first=False):
            pe.wait_ge(gl_gk, 32 * h + 32)
            if not first:
                pe.wait_ge(gl_on, h)
            for s in range(2):
                for c in range(2):
                    mm = pe.matmul(z_banks[2 * s + c][:, 0:TM], lgk[:, s, c * P:(c + 1) * P], lr,
                                   start=True, stop=True)
            mm.then_inc(gl_zp, 1)

        def gl_bias(dve, h):
            dve.wait_ge(gl_zp, h + 1)
            for s in range(2):
                for c in range(2):
                    ins = dve.tensor_scalar(lz[:, 2 * s + c], z_banks[2 * s + c][:, 0:TM],
                                            VA[:, bass.ds(V_GKB + 8 * s + c + 2 * h, 1)], None,
                                            ALU.add)
            ins.then_inc(gl_z, 1)

        def gl_logsig(act, h, first=False):
            act.wait_ge(gl_z, h + 1)
            if not first:
                act.wait_ge(gl_lo, h)
            act.activation(ll, lz, ACT.Abs).then_inc(gl_l, 1)
            act.wait_ge(gl_l, 3 * h + 1)
            act.activation(ll, ll, ACT.Exp, scale=-1.0).then_inc(gl_l, 1)
            act.wait_ge(gl_l, 3 * h + 2)
            act.activation(ll, ll, ACT.Ln, bias=1.0).then_inc(gl_l, 1)

        def gl_cumulate(dve, c, h):
            dve.wait_ge(gl_l, 3 * h + 3)
            c.link(dve.scalar_tensor_tensor(out=lz, in0=lz, scalar=0.0, in1=ll, op0=ALU.min,
                                            op1=ALU.subtract))
            for s in range(2):
                for k in range(2):
                    dve.tensor_tensor_scan(lcum[:, s, k, 1:T + 1], ones, lz[:, 2 * s + k, 0:T], 0.0,
                                           ALU.mult, ALU.add)
            for k in range(2):
                ins = dve.tensor_tensor_scan(lcm[:, k, :], ones[:, 0:META], lz[:, k, T:TM], 0.0,
                                             ALU.mult, ALU.add)
            c.link(ins)

        def gl_exponents(dve, c, h):
            for s in range(2):
                for n in range(GC):
                    r = (n + s) * GLA_C
                    ref = lambda N: lcum[:, s, :, r:r + 1].broadcast_to([P, 2, N])
                    q = lcum[:, s, :, n * GLA_C + 1 - s:(n + 1) * GLA_C + 1 - s]
                    k0, k1 = lkr[s][n]
                    k = lcum[:, s, :, k0 + 1 - s:k1 + 1 - s]
                    dq = lqd[:, s, :, n * GLA_C:(n + 1) * GLA_C]
                    dk = lk[:, s, n, :, k0:k1]
                    if s == 0:
                        dve.tensor_tensor(dq, q, ref(GLA_C), ALU.subtract)
                        dve.tensor_tensor(dk, ref(k1 - k0), k, ALU.subtract)
                        dve.tensor_tensor(lkm[:, n], ref(META), lcm, ALU.subtract)
                    else:
                        dve.tensor_tensor(dq, ref(GLA_C), q, ALU.subtract)
                        ins = dve.tensor_tensor(dk, k, ref(k1 - k0), ALU.subtract)
            c.link(ins)
            dve.tensor_tensor(lkm, lkm, lcm[:, :, META - 1:META].unsqueeze(1)
                              .broadcast_to([P, GC, 2, META]), ALU.add).then_inc(gl_ex, 1)

        def gl_exps(act, h):
            act.wait_ge(gl_ex, h + 1)
            act.activation(lqd, lqd, ACT.Exp, scale=1.0 / 16)
            for s in range(2):
                for n in range(GC):
                    k0, k1 = lkr[s][n]
                    act.activation(lk[:, s, n, :, k0:k1], lk[:, s, n, :, k0:k1], ACT.Exp,
                                   scale=1.0 / 16)
            act.activation(lkm, lkm, ACT.Exp, scale=1.0 / 16).then_inc(gl_exp, 1)

        def gl_decayed(dve, h):
            dve.wait_ge(gl_exp, h + 1)
            for s in range(2):
                dve.scalar_tensor_tensor(out=lqd[:, s], in0=lqk[:, 0:2, 0:T], scalar=1.0 / 16,
                                         in1=lqd[:, s], op0=ALU.mult, op1=ALU.mult)
                for n in range(GC):
                    k0, k1 = lkr[s][n]
                    dve.tensor_tensor(lk[:, s, n, :, k0:k1], lk[:, s, n, :, k0:k1],
                                      lqk[:, 2:4, k0:k1], ALU.mult)
            dve.tensor_tensor(lkm, lkm, lqk[:, 2:4, T:TM].unsqueeze(1)
                              .broadcast_to([P, GC, 2, META]), ALU.mult).then_inc(gl_m, 1)

        y = G[:, 0:KC * TM].rearrange("p (k n) -> p k n", n=TM)
        yr, ys = sem("y_added"), sem("y_scaled")

        def looped(eng, count, body):
            with eng.Fori(0, count - 1) as i:
                body(i, False)
            body(count - 1, True)

        def y_square(act, U0, c0, i, s, N):
            act.wait_ge(evacuated, U0 + s + 1 + 4 * i)
            act.wait_ge(c_acc, c0 + s + 4 * i - 1)
            apart(act)
            act.activation(SQ[:, s % 2, 0:N], ch(y, 4 * i + s, N), ACT.Square).then_inc(c_sq, 1)

        def y_evac(dve, U0, i, s, N):
            done(dve, U0 + s, 4, i)
            dve.tensor_copy(ch(y, 4 * i + s, N), psU[(U0 + s) % 2][:, 0:N]).then_inc(evacuated, 1)

        def y_scale(dve, kc, v, N):
            dve.scalar_tensor_tensor(out=ch(y, kc, N), in0=ch(y, kc, N),
                                     scalar=VA[:, bass.ds(v + kc, 1)], in1=RS[:, 0:N],
                                     op0=ALU.mult, op1=ALU.mult).then_inc(ys, 1)

        def y_add(pool, kc, c0, N, then):
            pool.wait_ge(ys, c0 + kc + 1)
            apart(pool)
            pool.tensor_tensor(ch(X, kc, N), ch(X, kc, N), ch(y, kc, N), ALU.add).then_inc(then, 1)

        def silu_gate(act, U0, i, s, N, then):
            act.wait_ge(evacuated, U0 + s + 1 + 4 * i)
            apart(act)
            g = G[:, bass.ds(N * (4 * i + s), N)]
            act.activation(g, g, ACT.Silu).then_inc(then, 1)

        def sp_second(sp):
            sp.wait_ge(c_lo, 32)
            sp.dma_start(con2, const[:, N_K:N_K + N_K2]).then_inc(s_con, 16)

            def chunks(U0, wv, c0):
                with sp.Fori(0, 4) as i:
                    for s in range(4):
                        load_unit(sp, U0 + s, 4, i, wv, c0 + P * s + 4 * P * i)

            chunks(U_AG, w_ai, 4096)
            with sp.Fori(0, GQ_KV) as j:
                for s, c in enumerate((2048 + P * j, 2 * P * j, P + 2 * P * j, 3072 + P * j)):
                    load_unit(sp, U_AT + s, 4, j, w_ai, c)
            chunks(U_AO, w_ao, 0)
            chunks(U_GG, w_gi, 4096)
            load_unit(sp, U_LR, 0, 0, w_gi, 6144, w=32)
            with sp.Fori(0, GLA_H) as h:
                for m in range(4):
                    load_unit(sp, U_GL + m, 8, h, w_gi, 2048 + P * m + 512 * h)
                for m in range(4):
                    load_unit(sp, U_GL + 4 + m, 8, h, w_gi, 1024 * (m // 2) + P * (m % 2) + 256 * h)
            chunks(U_GO, w_go, 0)

        def pe_second(pe):
            pe.wait_ge(c_lo, 48)
            mm_unit(pe, U_AG, 0, 0, BH, BL, TM)
            pe_norm(pe, 2, TM)
            for s in range(1, 4):
                mm_unit(pe, U_AG + s, 0, 0, BH, BL, TM)
            with pe.Fori(1, 4) as i:
                for s in range(4):
                    mm_unit(pe, U_AG + s, 4, i, BH, BL, TM)
            pe.wait_ge(s_con, 32)

            def head(j):
                first = isinstance(j, int)
                mm_unit(pe, U_AT, 4, j, BH, BL, TM)
                if not first:
                    ga_perm(pe, j - 1)
                mm_unit(pe, U_AT + 1, 4, j, BH, BL, TM)
                if not first:
                    ga_scores(pe, j - 1)
                mm_unit(pe, U_AT + 2, 4, j, BH, BL, TM)
                if not first:
                    ga_turn(pe, j - 1)
                mm_unit(pe, U_AT + 3, 4, j, BH, BL, TM)
                ga_ssq(pe, j, first)
                if not first:
                    ga_values(pe, j - 1)

            head(0)
            with pe.Fori(1, GQ_KV) as j:
                head(j)
            for stage in (ga_perm, ga_scores, ga_turn, ga_values):
                stage(pe, GQ_KV - 1)
            pe.wait_ge(aq_lo, GQ_KV)
            with pe.Fori(0, 4) as i:
                for s in range(4):
                    mm_unit(pe, U_AO + s, 4, i, AH, AL, TM)
            pe_norm(pe, 3, TM)

            dst = psU[U_GG % 2][:, 0:T]
            for h in range(2):
                pe.wait_ge(c_lo, 56 + 8 * h)
                mm_block(pe, U_GG, h, 0, 0, BH, BL, 8 * h, dst, T, start=h == 0, stop=h == 1)
            pe_norm(pe, 4, TM)
            for s in range(1, 4):
                mm_unit(pe, U_GG + s, 0, 0, BH, BL)
            with pe.Fori(1, 4) as i:
                for s in range(4):
                    mm_unit(pe, U_GG + s, 4, i, BH, BL)
            mm_unit(pe, U_LR, 0, 0, BH, BL, TM, w=32)

            def gla(h):
                first = isinstance(h, int)
                unit = lambda m: mm_unit(pe, U_GL + m, 8, h, BH, BL, TM)
                unit(0)
                if not first:
                    gl_scores(pe, h - 1)
                unit(1)
                if not first:
                    gl_out(pe, h - 1)
                gl_turn(pe, h, 0)
                unit(2)
                if not first:
                    gl_ssqs(pe, h - 1)
                gl_turn(pe, h, 1)
                unit(3)
                gl_turn(pe, h, 2)
                gl_logits(pe, h, first)
                unit(4)
                gl_turn(pe, h, 3)
                for m in range(5, 8):
                    unit(m)

            gla(0)
            with pe.Fori(1, GLA_H) as h:
                gla(h)
            for stage in (gl_scores, gl_out, gl_ssqs):
                stage(pe, GLA_H - 1)
            pe.wait_ge(gl_lo, GLA_H)
            with pe.Fori(0, 4) as i:
                for s in range(4):
                    mm_unit(pe, U_GO + s, 4, i, AH, AL)
            pe_norm(pe, 5, T)

        def act_second(act):
            split_hi(act, U_AG + 1, 0, 0)
            act_norm(act, 2, TM)
            silu_gate(act, U_AG, 0, 0, TM, ga_sg)
            for s in range(1, 4):
                split_hi(act, U_AG + s + 1, 0, 0)
                silu_gate(act, U_AG, 0, s, TM, ga_sg)
            with act.Fori(1, 4) as i:
                for s in range(4):
                    split_hi(act, U_AG + s + 1, 4, i)
                    silu_gate(act, U_AG, i, s, TM, ga_sg)

            def head(j):
                first = isinstance(j, int)
                split_hi(act, U_AT + 1, 4, j)
                if not first:
                    ga_copy_v(act, j - 1)
                split_hi(act, U_AT + 2, 4, j)
                if not first:
                    ga_exp(act, j - 1)
                split_hi(act, U_AT + 3, 4, j)
                if not first:
                    ga_copy_a(act, j - 1)
                act.wait_ge(evacuated, U_AT + 3 + 4 * j)
                ga_square(act, j)
                split_hi(act, U_AT + 4, 4, j)
                ga_root(act, j)

            head(0)
            with act.Fori(1, GQ_KV) as j:
                head(j)
            for stage in (ga_copy_v, ga_exp, ga_copy_a):
                stage(act, GQ_KV - 1)
            with act.Fori(0, 4) as i:
                for s in range(4):
                    split_hi(act, U_AO + s + 1, 4, i)
                    y_square(act, U_AO, 48, i, s, TM)
            split_hi(act, U_GG + 1, 0, 0)
            act_norm(act, 3, TM)
            with act.Fori(0, KC // 2) as i:
                for s in range(2):
                    kc = 2 * i + s
                    act.wait_ge(yr, kc + 1)
                    act_chunk(act, 48 + kc, kc, V_PRE + KC, BH, TM)
                    act_square(act, 64 + kc, s, kc, TM)

            act_norm(act, 4, TM)
            silu_gate(act, U_GG, 0, 0, T, gl_sg)
            for s in range(1, 4):
                split_hi(act, U_GG + s + 1, 0, 0)
                silu_gate(act, U_GG, 0, s, T, gl_sg)
            with act.Fori(1, 3) as i:
                for s in range(4):
                    split_hi(act, U_GG + s + 1, 4, i)
                    silu_gate(act, U_GG, i, s, T, gl_sg)
            for s in range(4):
                split_hi(act, U_GG + 13 + s, 0, 0, 32 * HB if s == 3 else P * HB)
                silu_gate(act, U_GG, 3, s, T, gl_sg)
            split_hi(act, U_LR + 1, 0, 0)
            act.wait_ge(gl_zero, 1)

            def gla(h):
                first = isinstance(h, int)
                split = lambda m: split_hi(act, U_GL + m, 8, h)
                gl_load(act, h)
                split(1)
                split(2)
                if not first:
                    gl_square(act, h - 1)
                gl_copy_v(act, h, 0)
                split(3)
                if not first:
                    gl_rootf(act, h - 1)
                gl_copy_v(act, h, 1)
                split(4)
                if not first:
                    gl_out_hi(act, h - 1)
                gl_copy_v(act, h, 2)
                split(5)
                gl_logsig(act, h, first)
                gl_copy_v(act, h, 3)
                split(6)
                split(7)
                gl_exps(act, h)
                split(8)

            gla(0)
            with act.Fori(1, GLA_H) as h:
                gla(h)
            for stage in (gl_square, gl_rootf, gl_out_hi):
                stage(act, GLA_H - 1)

            def y_slot(i, last):
                for s in range(4):
                    if not (last and s == 3):
                        split_hi(act, U_GO + s + 1, 4, i)
                    y_square(act, U_GO, 80, i, s, T)
            looped(act, 4, y_slot)
            act_norm(act, 5, T)

        def dve_second(dve):
            split_lo(dve, U_AG + 1, 0, 0)
            dve_norm(dve, 2, TM)
            done(dve, U_AG, 0, 0)
            evac(dve, U_AG, 0, 0, G[:, 0:TM], TM)
            for s in range(1, 4):
                split_lo(dve, U_AG + s + 1, 0, 0)
                done(dve, U_AG + s, 0, 0)
                evac(dve, U_AG + s, 0, 0, G[:, s * TM:(s + 1) * TM], TM)
            with dve.Fori(1, 4) as i:
                for s in range(4):
                    split_lo(dve, U_AG + s + 1, 4, i)
                    done(dve, U_AG + s, 4, i)
                    evac(dve, U_AG + s, 4, i, G[:, bass.ds(s * TM + 4 * TM * i, TM)], TM)
            dve.wait_ge(s_con, 32)
            dve.wait_ge(ga_sg, KC)
            ca = Chain(dve, ch_second)

            def head(j):
                first = isinstance(j, int)
                ca.begin(j, 2, O_GA - 2)
                split_lo(dve, U_AT + 1, 4, j)
                if not first:
                    ga_normed(dve, ca, j - 1)
                done(dve, U_AT, 4, j)
                evac(dve, U_AT, 4, j, aw[:, 0], TM)
                if not first:
                    ga_rope(dve, ca, j - 1)
                split_lo(dve, U_AT + 2, 4, j)
                done(dve, U_AT + 1, 4, j)
                evac(dve, U_AT + 1, 4, j, aw[:, 1], TM)
                if not first:
                    ga_min(dve, j - 1)
                if not first:
                    ga_weights(dve, ca, j - 1)
                split_lo(dve, U_AT + 3, 4, j)
                done(dve, U_AT + 2, 4, j)
                evac(dve, U_AT + 2, 4, j, aw[:, 2], TM)
                if not first:
                    ga_copy_d(dve, j - 1)
                split_lo(dve, U_AT + 4, 4, j)
                done(dve, U_AT + 3, 4, j)
                evac(dve, U_AT + 3, 4, j, avr, TM)
                if not first:
                    ga_gated(dve, j - 1)
                    ca.end()

            head(0)
            with dve.Fori(1, GQ_KV) as j:
                head(j)
            ca.begin(GQ_KV, 2, O_GA - 2)
            j = GQ_KV - 1
            ga_normed(dve, ca, j)
            ga_rope(dve, ca, j)
            ga_min(dve, j)
            ga_weights(dve, ca, j)
            ga_copy_d(dve, j)
            ga_gated(dve, j)
            with dve.Fori(0, 4) as i:
                for s in range(4):
                    split_lo(dve, U_AO + s + 1, 4, i)
                    y_evac(dve, U_AO, i, s, TM)
            split_lo(dve, U_GG + 1, 0, 0)
            dve_norm(dve, 3, TM)
            with dve.Fori(0, KC) as kc:
                y_scale(dve, kc, V_POST, TM)
            with dve.Fori(0, KC) as kc:
                dve_chunk(dve, 48 + kc, kc, V_PRE + KC, BH, BL, TM)

            dve_norm(dve, 4, TM)
            done(dve, U_GG, 0, 0)
            evac(dve, U_GG, 0, 0, G[:, 0:T])
            for s in range(1, 4):
                split_lo(dve, U_GG + s + 1, 0, 0)
                done(dve, U_GG + s, 0, 0)
                evac(dve, U_GG + s, 0, 0, G[:, s * T:(s + 1) * T])
            with dve.Fori(1, 3) as i:
                for s in range(4):
                    split_lo(dve, U_GG + s + 1, 4, i)
                    done(dve, U_GG + s, 4, i)
                    evac(dve, U_GG + s, 4, i, G[:, bass.ds(s * T + 4 * T * i, T)])
            for s in range(12, 16):
                split_lo(dve, U_GG + s + 1, 0, 0, 32 * HB if s == 15 else P * HB)
                done(dve, U_GG + s, 0, 0)
                evac(dve, U_GG + s, 0, 0, G[:, s * T:(s + 1) * T])
            split_lo(dve, U_LR + 1, 0, 0)
            done(dve, U_LR, 0, 0)
            evac(dve, U_LR, 0, 0, lr, TM, hi_p=32)
            dve.wait_ge(gl_sg, KC)
            dve.wait_ge(gl_zero, 1)
            cl = Chain(dve, ch_second)

            def gla(h):
                first = isinstance(h, int)
                cl.begin(h, *((3, O_GL) if first else (5, O_GL - 2)))
                def unit(m, dst):
                    done(dve, U_GL + m, 8, h)
                    evac(dve, U_GL + m, 8, h, dst, TM)
                split = lambda m: split_lo(dve, U_GL + m, 8, h)
                split(1)
                if not first:
                    dve.wait_ge(evacuated, U_GL + 8 * h)
                    gl_decayed(dve, h - 1)
                unit(0, lvr[:, 0])
                if not first:
                    gl_mask(dve, cl, h - 1)
                split(2)
                unit(1, lvr[:, 1])
                split(3)
                unit(2, lvr[:, 0])
                split(4)
                if not first:
                    gl_normed(dve, cl, h - 1)
                unit(3, lvr[:, 1])
                gl_bias(dve, h)
                split(5)
                if not first:
                    gl_out_lo(dve, h - 1)
                unit(4, lqk[:, 0])
                dve.wait_ge(gl_z, h + 1)
                gl_cumulate(dve, cl, h)
                split(6)
                unit(5, lqk[:, 1])
                gl_exponents(dve, cl, h)
                split(7)
                unit(6, lqk[:, 2])
                split(8)
                unit(7, lqk[:, 3])
                cl.end()

            gla(0)
            with dve.Fori(1, GLA_H) as h:
                gla(h)
            cl.begin(0, 2, O_GL + 5 * GLA_H - 2)
            h = GLA_H - 1
            dve.wait_ge(evacuated, U_GO)
            gl_decayed(dve, h)
            gl_mask(dve, cl, h)
            gl_normed(dve, cl, h)
            gl_out_lo(dve, h)

            def y_slot(i, last):
                for s in range(4):
                    if not (last and s == 3):
                        split_lo(dve, U_GO + s + 1, 4, i)
                    y_evac(dve, U_GO, i, s, T)
            looped(dve, 4, y_slot)
            dve_norm(dve, 5, T)
            with dve.Fori(0, KC) as kc:
                y_scale(dve, kc, V_POST + KC, T)

        def pool_second(pool):
            def squares(c0, N):
                for s in range(4):
                    pool_square(pool, c0 + s, s % 2, N, s == 0)
                with pool.Fori(1, 4) as i:
                    for s in range(4):
                        pool_square(pool, c0 + 4 * i + s, s % 2, N)

            with pool.Fori(0, GQ_KV) as j:
                ga_split(pool, j)
            squares(48, TM)
            with pool.Fori(0, KC) as kc:
                y_add(pool, kc, 0, TM, yr)
            squares(64, TM)
            pool.wait_ge(s_nrm, 5)
            for dst in (lk[:, 0, 0, :, GLA_C:P], lk[:, 0, 2, :, 3 * GLA_C:T], lk[:, 1, 1, :, 0:GLA_C],
                        lk[:, 1, 3, :, P:3 * GLA_C], lcum[:, :, :, 0:1]):
                pool.memset(dst, 0.0)
            pool.memset(lgk, 0.0).then_inc(gl_zero, 1)
            squares(80, T)
            with pool.Fori(0, KC) as kc:
                y_add(pool, kc, KC, T, x_final)

        block = ctx.enter_context(nc.Block())

        @block.sync
        def _(sp):
            sp.dma_start(con[:, :], const[:, 0:N_K]).then_inc(s_con, 16)
            for v, name in ((V_ATTN, "norm_attn"), (V_FFN, "norm_ffn"), (V_PRE, "pre_norm_2"),
                            (V_POST, "post_norm_2"), (V_GKB, "gla_gk_bias_2"),
                            (V_ON, "gla_o_norm_2")):
                src = a[name] if name != "gla_gk_bias_2" else a[name][0]
                src = src.rearrange("a (r c) -> (a r) c", c=P)
                sp.dma_start(va_in[v:v + src.shape[0], :], src).then_inc(s_va, 16)
            for v, name in ((V_FQ, "fox_q_gain"), (V_FK, "fox_k_gain"), (V_NQ, "nsa_q_gain"),
                            (V_KC, "nsa_kc_gain"), (V_KS, "nsa_ks_gain"), (V_KW, "nsa_kw_gain"),
                            (V_AQ, "attn_q_norm_2"), (V_AK, "attn_k_norm_2")):
                sp.dma_start(va_in[v:v + 1, :], a[name][:, 0:P]).then_inc(s_va, 16)
            sp.wait_ge(s_vbz, 1)
            sp.dma_start(vb_in[V_PEK:V_PEK + 32, :], a["cmp_pe_k"][0][:, 0:P]).then_inc(s_vb, 16)
            sp.dma_start(vb_in[V_PEV:V_PEV + 32, :], a["cmp_pe_v"][0]).then_inc(s_vb, 16)
            sp.dma_start(vb_in[V_PET:V_PET + 32, 0:64], a["cmp_pe_k"][0][:, P:NSA_DK]).then_inc(s_vb, 16)
            for n, name in enumerate(("nsa_q_gain", "nsa_kc_gain", "nsa_ks_gain", "nsa_kw_gain")):
                sp.dma_start(vb_in[V_TQ + n:V_TQ + n + 1, 0:64], a[name][:, P:NSA_DK]).then_inc(s_vb, 16)
            sp.dma_start(w2k, a["cmp_w2_k"][0].rearrange("(h p) d -> p h d", p=P)).then_inc(w2_full, 16)
            sp.dma_start(w2v, a["cmp_w2_v"][0].rearrange("(h p) d -> p h d", p=P)).then_inc(w2_full, 16)

            load_unit(sp, U_B0, 0, 0, w_in, C_F, w=8, first=True)
            load_unit(sp, U_B0 + 1, 0, 0, w_in, C_NG, w=24, first=True)

            def fox(h):
                for s, c in enumerate((C_FQ, C_FK, C_FV, C_GATES)):
                    load_unit(sp, U_FOX + s, 4, h, w_in, c + P * h, first=isinstance(h, int))

            fox(0)
            with sp.Fori(1, FOX_H) as h:
                fox(h)
            U = U_NKV
            for ck, cv in ((C_KC, C_VC), (C_KS, C_VS), (C_KW, C_VW)):
                load_unit(sp, U, 0, 0, w_in, ck)
                load_unit(sp, U + 1, 0, 0, w_in, ck + NSA_DK)
                load_tails(sp, U + 2, 0, 0, ck)
                load_unit(sp, U + 3, 0, 0, w_in, cv)
                load_unit(sp, U + 4, 0, 0, w_in, cv + P)
                U += 5
            with sp.Fori(0, 4) as i:
                c = C_NQ + 2 * NSA_DK * i
                load_unit(sp, U_NQ, 4, i, w_in, c)
                load_unit(sp, U_NQ + 1, 4, i, w_in, c + NSA_DK)
                load_tails(sp, U_NQ + 2, 4, i, c)
                load_unit(sp, U_NQ + 3, 4, i, w_in, C_GATES + P * 8 + P * i)
            with sp.Fori(0, 5) as i:
                for s in range(4):
                    load_unit(sp, U_GATE + s, 4, i, w_in, C_GATES + P * 12 + P * s + 4 * P * i)
            with sp.Fori(0, 4) as i:
                for s in range(4):
                    c = P * s + 4 * P * i
                    load_block(sp, U_UP + s, 0, 4, i, w_upf[:, :, bass.ds(c, P)])
                    load_block(sp, U_UP + s, 1, 4, i, w_upn[:, :, bass.ds(c, P)])
            with sp.Fori(0, 4) as i:
                for s in range(4):
                    load_unit(sp, U_OUT + s, 4, i, w_o1, P * s + 4 * P * i)
            for (h0, n_h), (ug, ud) in zip(PASSES, u_ffn):
                with sp.Fori(0, n_h // 2) as i:
                    for s in range(2):
                        c = P * (h0 + s) + 2 * P * i
                        load_unit(sp, ug + 2 * s, 4, i, w_fg, c)
                        load_unit(sp, ug + 2 * s + 1, 4, i, w_fu, c)
                with sp.Fori(0, 4) as i:
                    for s in range(4):
                        load_unit(sp, ud + s, 4, i, w_fd[:, h0:h0 + n_h], P * s + 4 * P * i, kb=n_h // 2)
            sp_second(sp)
            for n in range(4):
                sp.wait_ge(o_c, 4 * n + 4)
                sp.dma_start(out[:, 512 * n:512 * n + 512].rearrange("(t p) d -> p t d", p=P),
                             otok[:, :, 512 * n:512 * n + 512]).then_inc(s_out[n % 2], 16)
            for s in s_out:
                sp.wait_ge(s, 32)

        @block.tensor
        def _(pe):
            pe.wait_ge(s_con, 16)
            pe.wait_ge(s_va, 16 * 14)
            pe.wait_ge(s_vb, 16 * 7)
            pe.transpose(psT[0][:, 0:N_VA], va_in[0:N_VA, :], ident[0:N_VA, 0:N_VA])
            pe.transpose(psT[0][:, P:P + N_VB], vb_in[0:N_VB, :], ident[0:N_VB, 0:N_VB]).then_inc(s_vt, 1)
            pe.wait_ge(s_x, 32)
            for kc in range(KC):
                if kc >= 4:
                    pe.wait_ge(c_x, kc - 3)
                for t in range(2):
                    pe.transpose(x_banks[kc % 4][:, t * P:(t + 1) * P],
                                 xtok[:, t, kc * P:(kc + 1) * P], ident)
                pe.transpose(x_banks[kc % 4][:, T:TM], mtok[:, kc * P:(kc + 1) * P],
                             ident[0:META, 0:META]).then_inc(s_xt, 1)

            pe.wait_ge(c_lo, 16)
            mm_unit(pe, U_B0, 0, 0, AH, AL, w=8)
            pe_norm(pe, 0, T)
            mm_unit(pe, U_B0 + 1, 0, 0, AH, AL, w=24)

            def fox(h):
                first = isinstance(h, int)
                u = [(U_FOX + s, 4, h) for s in range(4)]
                mm_unit(pe, *u[0], AH, AL)
                if not first:
                    fox_scores(pe, h - 1)
                mm_unit(pe, *u[1], AH, AL)
                if not first:
                    fox_turn(pe, h - 1)
                mm_unit(pe, *u[2], AH, AL)
                if not first:
                    fox_values(pe, h - 1)
                else:
                    pe.wait_ge(s_rs, 2)
                fox_ssq(pe, h, first)
                mm_unit(pe, *u[3], AH, AL)
                pe.wait_ge(evacuated, U_FOX + 3 + 4 * h)
                if not first:
                    pe.wait_ge(fx_v, h)
                for t in range(2):
                    mm = pe.transpose(psT[1][:, t * P:(t + 1) * P], vr[:, t * P:(t + 1) * P], ident)
                mm.then_inc(fx_vt, 1)

            pe.wait_ge(evacuated, U_B0 + 2)
            for t in range(2):
                mm = pe.transpose(psT[1][:, 32 * t:32 * t + 24], fz[:, 2, t * P:(t + 1) * P],
                                  ident[0:24, 0:24])
            mm.then_inc(ng_t, 1)
            pe.wait_ge(ng_c, 1)
            fox(0)
            with pe.Fori(1, FOX_H) as h:
                fox(h)

            pieces = iter(range(len(CPIECES)))
            for st in range(3):
                for s in range(5):
                    U, slot = U_NKV + 5 * st + s, 5 * st + s
                    mm_unit(pe, U, 0, 0, AH, AL)
                    if slot == 0:
                        fox_scores(pe, FOX_H - 1)
                    elif slot == 1:
                        fox_turn(pe, FOX_H - 1)
                    elif slot == 2:
                        fox_values(pe, FOX_H - 1)
                    if st and s == 3:
                        pe.wait_ge(nk_sq, st)
                        if st == 1:
                            pe.wait_ge(fx_nrm, 2 * FOX_H)
                        else:
                            pe.wait_ge(nk_nrm, 2)
                        pe.matmul(psN[:, :], i192, ksq, start=True, stop=False)
                        pe.matmul(psN[:, :], i192[0:64, :], ktsq, start=False, stop=True)\
                          .then_inc(nk_ssq, 1)
                    if slot in (9, 10, 14):
                        nsa_turn_v(pe, (9, 10, 14).index(slot), U - 1)
                    if slot >= 4:
                        for _ in range(2):
                            m = next(pieces)
                            if m == 0:
                                pe.wait_ge(fx_olo, FOX_H)
                            cmp_piece(pe, m)
            for m in pieces:
                cmp_piece(pe, m)

            def pair(i):
                first = isinstance(i, int)
                g = 0 if first else (i - 1) // 2
                n = 0 if first else 2 * (i - 1)
                mm_unit(pe, U_NQ, 4, i, AH, AL)
                if first:
                    nsa_turn_v(pe, 3, U_NQ - 1)
                else:
                    pe.wait_ge(nq_q, i)
                    nsa_scores(pe, n, g, 0)
                mm_unit(pe, U_NQ + 1, 4, i, AH, AL)
                if first:
                    pe.wait_ge(cm_hs, 1)
                    pe.wait_ge(w2_full, 32)
                    pe.wait_ge(nk_nrm, 4)
                    for v, dst, wgt in ((0, psN[:, 0:30], w2k[:, :, 0:P]),
                                        (0, psN[0:64, 32:62], w2k[:, :, P:NSA_DK])):
                        for h in range(2):
                            pe.matmul(dst, wgt[:, h], hsl[:, v, h, :], start=h == 0, stop=h == 1)
                    for g_ in range(2):
                        for h in range(2):
                            mm = pe.matmul(psN[0:NB_C, 64 + P * g_:64 + P * (g_ + 1)],
                                           hsl[:, 1, h, g_ * NB_C:(g_ + 1) * NB_C], w2v[:, h],
                                           start=h == 0, stop=h == 1)
                    mm.then_inc(cm_kc, 1)
                else:
                    nsa_turn(pe, n)
                    nsa_scores(pe, n + 1, g, 1)
                mm_unit(pe, U_NQ + 2, 4, i, AH, AL)
                if first:
                    pe.wait_ge(cm_sq, 1)
                    pe.matmul(psN[:, 320:350], i192, kcs, start=True, stop=False)
                    pe.matmul(psN[:, 320:350], i192[0:64, :], kcts, start=False, stop=True)\
                      .then_inc(cm_ms, 1)
                else:
                    pe.wait_ge(na_vc, i)
                    nsa_values(pe, n, 0)
                    nsa_turn(pe, n + 1)
                mm_unit(pe, U_NQ + 3, 4, i, AH, AL)
                if first:
                    pe.wait_ge(cm_rs, 2)
                else:
                    nsa_values(pe, n + 1, 1)
                pe.wait_ge(nq_sq, 2 * i + 2)
                if not first:
                    pe.wait_ge(nq_nrm, 2 * i)
                pe.matmul(psN[:, :], i192, nsq, start=True, stop=False)
                pe.matmul(psN[:, :], i192[0:64, :], qt_sq, start=False, stop=True).then_inc(nq_ssq, 1)

            pair(0)
            with pe.Fori(1, 4) as i:
                pair(i)

            mm_unit(pe, U_GATE, 4, 0, AH, AL)
            pe.wait_ge(nq_q, 4)
            nsa_scores(pe, 6, 1, 0)
            mm_unit(pe, U_GATE + 1, 4, 0, AH, AL)
            nsa_turn(pe, 6)
            nsa_scores(pe, 7, 1, 1)
            mm_unit(pe, U_GATE + 2, 4, 0, AH, AL)
            pe.wait_ge(na_vc, 4)
            nsa_values(pe, 6, 0)
            nsa_turn(pe, 7)
            mm_unit(pe, U_GATE + 3, 4, 0, AH, AL)
            nsa_values(pe, 7, 1)
            with pe.Fori(1, 5) as i:
                for s in range(4):
                    mm_unit(pe, U_GATE + s, 4, i, AH, AL)

            pe.wait_ge(na_olo, NSA_H)
            with pe.Fori(0, 4) as i:
                for s in range(4):
                    U = U_UP + s
                    mm_block(pe, U, 0, 4, i, BH, BL, 0, psU[U % 2][:, 0:T], T)
                    mm_block(pe, U, 1, 4, i, BH, BL, 8, psU[U % 2][:, T:2 * T], T)
            pe.wait_ge(up_lo, 16)
            with pe.Fori(0, 4) as i:
                for s in range(4):
                    mm_unit(pe, U_OUT + s, 4, i, AH, AL)

            for (h0, n_h), (ug, ud) in zip(PASSES, u_ffn):
                def hidden(i, norm=False):
                    for s in range(4):
                        mm_unit(pe, ug + s, 4, i, BH, BL)
                        if norm and s == 0:
                            pe_norm(pe, 1, T)
                if h0 == 0:
                    pe.wait_ge(c_lo, 32)
                    hidden(0, True)
                    with pe.Fori(1, n_h // 2) as i:
                        hidden(i)
                else:
                    with pe.Fori(0, n_h // 2) as i:
                        hidden(i)
                pe.wait_ge(ff_lo, h0 + n_h)
                with pe.Fori(0, 4) as i:
                    for s in range(4):
                        mm_unit(pe, ud + s, 4, i, AH, AL, kb=n_h // 2)

            pe_second(pe)

            for n in range(8):
                pe.wait_ge(x_final, 2 * n + 2)
                for t in range(2):
                    k = 2 * n + t
                    if k >= 4:
                        pe.wait_ge(o_c, k - 3)
                    for q in range(2):
                        mm = pe.transpose(x_banks[k % 4][:, q * P:(q + 1) * P],
                                          X[:, 2 * n + q, t * P:(t + 1) * P], ident)
                    mm.then_inc(o_t, 1)

        @block.scalar
        def _(act):
            act.dma_start(xtok, a["x"][0].rearrange("(t p) d -> p t d", p=P)).then_inc(s_x, 16)
            act.dma_start(mtok, a["meta_tokens_2"]).then_inc(s_x, 16)
            act.dma_start(fbias[:, :], a["fox_f_bias"].rearrange("a h -> h a")).then_inc(s_fb, 16)
            act.wait_ge(s_v, 1)
            for kc in range(KC):
                act.wait_ge(c_x, kc + 1)
                act_chunk(act, kc, kc, V_ATTN, AH, T)
                act_square(act, kc, kc % 2, kc, T, wait=kc >= 2)
            split_hi(act, U_B0, 0, 0, 8 * HB)
            split_hi(act, U_B0 + 1, 0, 0, 24 * HB)
            split_hi(act, U_FOX, 4, 0)
            act_norm(act, 0, T)
            act.wait_ge(fx_z, 1)
            act.activation(fz[0:FOX_H, 1], fz[0:FOX_H, 0], ACT.Abs).then_inc(fx_za, 1)
            act.wait_ge(fx_za, 1)
            act.activation(fz[0:FOX_H, 1], fz[0:FOX_H, 1], ACT.Exp, scale=-1.0).then_inc(fx_za, 1)
            act.wait_ge(fx_za, 2)
            act.activation(fz[0:FOX_H, 1], fz[0:FOX_H, 1], ACT.Ln, bias=1.0).then_inc(fx_za, 1)
            act.wait_ge(ng_c, 1)
            act.activation(gtok[:, :, :], gtok[:, :, :], ACT.Sigmoid).then_inc(ng_s, 1)

            def fox(h):
                first = isinstance(h, int)
                split_hi(act, U_FOX + 1, 4, h)
                fox_square(act, h, U_FOX, 4, 0, qr)
                if not first:
                    fox_exp(act, h - 1)
                split_hi(act, U_FOX + 2, 4, h)
                if not first:
                    fox_copy_pt(act, h - 1)
                fox_square(act, h, U_FOX + 1, 4, 1, kr)
                split_hi(act, U_FOX + 3, 4, h)
                if not first:
                    fox_out_hi(act, h - 1)
                fox_root(act, h)
                split_hi(act, U_FOX + 4, 4, h)
                act.wait_ge(fx_vt, h + 1)
                act.activation(fv, psT[1][:, 0:T].rearrange("p (t d) -> p t d", t=2), ACT.Copy)\
                   .then_inc(fx_v, 1)

            fox(0)
            with act.Fori(1, FOX_H) as h:
                fox(h)

            for slot in range(15):
                U = U_NKV + slot
                split_hi(act, U + 1, 0, 0, tails=1 if slot in (1, 6, 11) else None)
                if slot == 0:
                    fox_exp(act, FOX_H - 1)
                elif slot == 1:
                    fox_copy_pt(act, FOX_H - 1)
                elif slot == 2:
                    fox_out_hi(act, FOX_H - 1)
                if slot in (7, 12):
                    act.wait_ge(evacuated, U + 1)
                    if slot == 12:
                        act.wait_ge(nk_k, 1)
                    act.activation(ksq, kraw.rearrange("p a n -> p (a n)"), ACT.Square)
                    act.activation(ktsq, ktraw.rearrange("p a n -> p (a n)"), ACT.Square)\
                       .then_inc(nk_sq, 1)
                if slot in (8, 13):
                    act.wait_ge(nk_ssq, slot // 5)
                    root_rms(act, ksq, psN[:, :], nk_nrm, slot // 5 - 1)
                if slot in (9, 10, 14):
                    nsa_copy_v(act, (9, 10, 14).index(slot))

            def pair(i):
                first = isinstance(i, int)
                n = 0 if first else 2 * (i - 1)
                split_hi(act, U_NQ + 1, 4, i)
                if first:
                    nsa_copy_v(act, 3)
                    act.wait_ge(cw_used, len(CPIECES))
                    for v in range(2):
                        for h in range(2):
                            ins = act.activation(hsl[:, v, h, :], cmp_banks[2 * v + h][:, 0:30], ACT.Silu)
                    ins.then_inc(cm_hs, 1)
                else:
                    nsa_exp(act, n)
                split_hi(act, U_NQ + 2, 4, i, tails=i + 1)
                if first:
                    act.wait_ge(cm_kcr, 1)
                    act.activation(kcs, kcr, ACT.Square)
                    act.activation(kcts, kctr, ACT.Square).then_inc(cm_sq, 1)
                    act.wait_ge(evacuated, U_NQ + 2)
                    act.activation(nsq, qmr.rearrange("p a n -> p (a n)"), ACT.Square).then_inc(nq_sq, 1)
                else:
                    nsa_copy_a(act, n)
                    act.wait_ge(evacuated, U_NQ + 4 * i + 2)
                    act.activation(nsq, qmr.rearrange("p a n -> p (a n)"), ACT.Square).then_inc(nq_sq, 1)
                    nsa_exp(act, n + 1)
                split_hi(act, U_NQ + 3, 4, i)
                if first:
                    act.wait_ge(cm_ms, 1)
                    root_rms(act, kcrs, psN[:, 320:350], cm_rs, 0)
                else:
                    nsa_out_hi(act, n)
                    nsa_copy_a(act, n + 1)
                act.wait_ge(evacuated, U_NQ + 4 * i + 3)
                act.activation(qt_sq, qtr.rearrange("p a n -> p (a n)"), ACT.Square).then_inc(nq_sq, 1)
                split_hi(act, U_NQ + 4, 4, i)
                if not first:
                    nsa_out_hi(act, n + 1)
                act.wait_ge(nq_ssq, i + 1)
                root_rms(act, nsq, psN[:, :], nq_nrm, i)

            pair(0)
            with act.Fori(1, 4) as i:
                pair(i)
            split_hi(act, U_GATE + 1, 4, 0)
            nsa_exp(act, 6)
            split_hi(act, U_GATE + 2, 4, 0)
            nsa_copy_a(act, 6)
            nsa_exp(act, 7)
            split_hi(act, U_GATE + 3, 4, 0)
            nsa_out_hi(act, 6)
            nsa_copy_a(act, 7)
            split_hi(act, U_GATE + 4, 4, 0)
            nsa_out_hi(act, 7)
            with act.Fori(1, 5) as i:
                for s in range(4):
                    split_hi(act, U_GATE + s + 1, 4, i)

            act.wait_ge(evacuated, U_UP)
            with act.Fori(0, 4) as i:
                for s in range(4):
                    j = 4 * i + s
                    act.activation(gates(j), gates(j), ACT.Sigmoid).then_inc(up_sg, 1)
                    split_hi(act, U_UP + s + 1, 4, i)
                    act.wait_ge(up_mr, j + 1)
                    apart(act)
                    act.activation(ch(AH, j, T), up_m, ACT.Copy).then_inc(up_hi, 1)
            with act.Fori(0, 4) as i:
                for s in range(4):
                    split_hi(act, U_OUT + s + 1, 4, i)
                    act.wait_ge(evacuated, U_OUT + s + 1 + 4 * i)
                    act_chunk(act, 16 + s + 4 * i, 4 * i + s, V_FFN, BH, T)
                    act_square(act, 16 + s + 4 * i, s % 2, 4 * i + s, T)
            for (h0, n_h), (ug, ud) in zip(PASSES, u_ffn):
                def hidden(i, norm=False):
                    for s in range(2):
                        split_hi(act, ug + 2 * s + 1, 4, i)
                        if norm and s == 0:
                            act_norm(act, 1, T)
                        act.wait_ge(evacuated, ug + 2 * s + 1 + 4 * i)
                        act.activation(gsl[:, s], gsl[:, s], ACT.Silu).then_inc(ff_silu, 1)
                        split_hi(act, ug + 2 * s + 2, 4, i)
                        act.wait_ge(ff_h, h0 + s + 1 + 2 * i)
                        apart(act)
                        act.activation(ch(AH, 2 * i + s, T), hpr, ACT.Copy).then_inc(ff_hi, 1)
                if h0 == 0:
                    hidden(0, True)
                with act.Fori(1 if h0 == 0 else 0, n_h // 2) as i:
                    hidden(i)
                with act.Fori(0, 4) as i:
                    for s in range(4):
                        split_hi(act, ud + s + 1, 4, i)
                        if h0 == PASSES[-1][0]:
                            act.wait_ge(evacuated, ud + s + 1 + 4 * i)
                            act_chunk(act, 32 + s + 4 * i, 4 * i + s, V_PRE, BH, TM)
                            act_square(act, 32 + s + 4 * i, s % 2, 4 * i + s, TM)
            act_second(act)

        @block.vector
        def _(dve):
            st = Chain(dve, ch_start)
            st.begin(0, 6, 0)
            dve.memset(vb_in, 0.0).then_inc(s_vbz, 1)
            dve.wait_ge(s_vt, 1)
            dve.tensor_copy(VA[:, :], psT[0][:, 0:N_VA])
            st.link(dve.tensor_copy(VB[:, :], psT[0][:, P:P + N_VB]))
            for v, d in ((V_FQ, FOX_D), (V_NQ, NSA_DK), (V_AQ, GQ_D)):
                dve.tensor_scalar(VA[:, v:v + 1], VA[:, v:v + 1], -float(d) ** -0.5, None, ALU.mult)
            dve.tensor_scalar(VB[:, V_TQ:V_TQ + 1], VB[:, V_TQ:V_TQ + 1], -float(NSA_DK) ** -0.5,
                              None, ALU.mult).then_inc(s_v, 1)
            dve.wait_ge(s_v, 1)
            for kc in range(KC):
                dve.wait_ge(s_xt, kc + 1)
                dve.tensor_copy(X[:, kc, :], x_banks[kc % 4][:, 0:TM]).then_inc(c_x, 1)
                if kc:
                    dve_chunk(dve, kc - 1, kc - 1, V_ATTN, AH, AL, T)
            dve_chunk(dve, KC - 1, KC - 1, V_ATTN, AH, AL, T)
            split_lo(dve, U_B0, 0, 0, 8 * HB)
            split_lo(dve, U_B0 + 1, 0, 0, 24 * HB)
            split_lo(dve, U_FOX, 4, 0)
            dve_norm(dve, 0, T)
            done(dve, U_B0, 0, 0)
            evac(dve, U_B0, 0, 0, fz[0:FOX_H, 2], hi_p=FOX_H)
            dve.wait_ge(evacuated, U_B0 + 1)
            dve.wait_ge(s_fb, 16)
            z, zl, zm = fz[0:FOX_H, 0], fz[0:FOX_H, 1], fz[0:FOX_H, 2]
            dve.tensor_scalar(z, zm, fbias[:, 0:1], None, ALU.add).then_inc(fx_z, 1)
            dve.wait_ge(fx_z, 1)
            dve.wait_ge(fx_za, 3)
            st.link(dve.tensor_scalar(zm, z, 0.0, None, ALU.min))
            st.link(dve.tensor_tensor(zm, zm, zl, ALU.subtract))
            st.link(dve.tensor_tensor_scan(c_row[:, 0, :], ones[0:FOX_H, :], zm, 0.0, ALU.mult, ALU.add))
            st.link(dve.tensor_scalar(c_row[:, 1, :], c_row[:, 0, :], -1.0, None, ALU.mult))
            done(dve, U_B0 + 1, 0, 0)
            evac(dve, U_B0 + 1, 0, 0, fz[:, 2, :], hi_p=24)
            dve.wait_ge(ng_t, 1)
            dve.tensor_copy(gtok[:, :, :], psT[1][:, 0:64].rearrange("p (t n) -> p t n", t=2)[:, :, 0:24])\
               .then_inc(ng_c, 1)

            cf = Chain(dve, ch_fox)

            def fox(h):
                first = isinstance(h, int)
                u = [U_FOX + s for s in range(4)]
                cf.begin(h, 1, -1)
                split_lo(dve, u[1], 4, h)
                done(dve, u[0], 4, h)
                if not first:
                    dve.wait_ge(fx_qk, 2 * h)
                evac(dve, u[0], 4, h, qr)
                if not first:
                    fox_softmax(dve, cf, h - 1)
                if not first:
                    fox_weights(dve, cf, h - 1)
                split_lo(dve, u[2], 4, h)
                done(dve, u[1], 4, h)
                evac(dve, u[1], 4, h, kr)
                split_lo(dve, u[3], 4, h)
                done(dve, u[2], 4, h)
                evac(dve, u[2], 4, h, vr)
                if not first:
                    fox_out_lo(dve, h - 1)
                split_lo(dve, u[3] + 1, 4, h)
                fox_normed(dve, h)
                fox_decay(dve, h)
                done(dve, u[3], 4, h)
                evac(dve, u[3], 4, h, G[:, bass.ds(T * h, T)])
                if not first:
                    cf.end()

            fox(0)
            with dve.Fori(1, FOX_H) as h:
                fox(h)

            dve.wait_ge(ng_s, 1)
            gt = gtok[:, :, :].rearrange("p t (n b) -> p b n t", b=3)
            for k, b in enumerate((1, 2, 0)):
                ins = dve.tensor_copy(gtr[:, :, 2 * k:2 * k + 2], gt[:, b])
            st.link(ins)
            st.end()

            cf.begin(FOX_H, 1, -1)
            for slot in range(15):
                U, g, k = U_NKV + slot, slot % 5, slot // 5
                split_lo(dve, U + 1, 0, 0)
                if slot == 1:
                    fox_weights(dve, cf, FOX_H - 1)
                done(dve, U, 0, 0)
                if slot == 0:
                    dve.wait_ge(fx_qk, 2 * FOX_H)
                    dve.wait_ge(fx_vt, FOX_H)
                if slot == 10:
                    dve.wait_ge(nk_k, 1)
                if slot == 5:
                    dve.wait_ge(cp_ready, 2)
                if slot == 8:
                    dve.wait_ge(cp_ready, 3)
                if g < 2:
                    evac(dve, U, 0, 0, kraw[:, g])
                elif g == 2:
                    evac(dve, U, 0, 0, ktraw[:, 0], hi_p=64, last=False)
                    evac(dve, U, 0, 0, ktraw[:, 1], lo_p=64)
                else:
                    evac(dve, U, 0, 0, vraw[:, g - 3])
                if slot == 0:
                    fox_softmax(dve, cf, FOX_H - 1)
                if slot == 2:
                    fox_out_lo(dve, FOX_H - 1)
                if slot in (8, 13):
                    km, kt = ((ksm, kst), (kwm, kwt))[k - 1]
                    invert_root(dve, ksq, nk_nrm, k - 1)
                    dve.scalar_tensor_tensor(out=km, in0=kraw, scalar=VA[:, V_KC + k:V_KC + k + 1],
                                             in1=ksq.rearrange("p (a n) -> p a n", a=2),
                                             op0=ALU.mult, op1=ALU.mult)
                    dve.scalar_tensor_tensor(out=kt, in0=ktraw,
                                             scalar=VB[0:64, V_TQ + 1 + k:V_TQ + 2 + k],
                                             in1=ksq[0:64, :].rearrange("p (a n) -> p a n", a=2),
                                             op0=ALU.mult, op1=ALU.mult).then_inc(nk_k, 1)

            ca, cb = Chain(dve, ch_nq[0]), Chain(dve, ch_nq[1])

            def nq_norm(i):
                invert_root(dve, nsq, nq_nrm, i)
                dve.scalar_tensor_tensor(out=qm, in0=qmr, scalar=VA[:, V_NQ:V_NQ + 1],
                                         in1=nsq.rearrange("p (a n) -> p a n", a=2),
                                         op0=ALU.mult, op1=ALU.mult)
                dve.scalar_tensor_tensor(out=qt, in0=qtr, scalar=VB[0:64, V_TQ:V_TQ + 1],
                                         in1=nsq[0:64, :].rearrange("p (a n) -> p a n", a=2),
                                         op0=ALU.mult, op1=ALU.mult).then_inc(nq_q, 1)

            def pair(i):
                first = isinstance(i, int)
                n = 0 if first else 2 * (i - 1)
                u = [U_NQ + s for s in range(4)]
                ca.begin(i, 8, -8)
                cb.begin(i, 8, -8)
                split_lo(dve, u[1], 4, i)
                done(dve, u[0], 4, i)
                if first:
                    dve.wait_ge(nk_k, 2)
                else:
                    dve.wait_ge(nq_q, i)
                evac(dve, u[0], 4, i, qmr[:, 0])
                if not first:
                    nsa_softmax(dve, ca, n)
                if not first:
                    nsa_weights(dve, ca, n)
                split_lo(dve, u[2], 4, i)
                done(dve, u[1], 4, i)
                evac(dve, u[1], 4, i, qmr[:, 1])
                if first:
                    dve.wait_ge(cm_kc, 1)
                    dve.tensor_copy(kcr, psN[:, 0:30])
                    dve.tensor_copy(kctr, psN[0:64, 32:62])
                    dve.tensor_copy(vc_t, psN[0:NB_C, 64:320].rearrange("p (g d) -> p g d", g=2))\
                       .then_inc(cm_kcr, 1)
                else:
                    nsa_copy_d(dve, n)
                    nsa_softmax(dve, cb, n + 1)
                if not first:
                    nsa_weights(dve, cb, n + 1)
                split_lo(dve, u[3], 4, i)
                done(dve, u[2], 4, i)
                evac(dve, u[2], 4, i, qtr[:, 0], hi_p=64, last=False)
                evac(dve, u[2], 4, i, qtr[:, 1], lo_p=64)
                if first:
                    invert_root(dve, kcrs, cm_rs, 0)
                    dve.scalar_tensor_tensor(out=kcm, in0=kcr, scalar=VA[:, V_KC:V_KC + 1], in1=kcrs,
                                             op0=ALU.mult, op1=ALU.mult)
                    dve.scalar_tensor_tensor(out=kct, in0=kctr, scalar=VB[0:64, V_TQ + 1:V_TQ + 2],
                                             in1=kcrs[0:64, :], op0=ALU.mult, op1=ALU.mult)
                else:
                    nsa_out_lo(dve, n)
                    nsa_copy_d(dve, n + 1)
                split_lo(dve, u[3] + 1, 4, i)
                done(dve, u[3], 4, i)
                evac(dve, u[3], 4, i, G[:, bass.ds(8 * T + T * i, T)])
                nq_norm(i)
                if not first:
                    nsa_out_lo(dve, n + 1)
                    ca.end()
                    cb.end()

            pair(0)
            with dve.Fori(1, 4) as i:
                pair(i)

            ca.begin(4, 8, -8)
            cb.begin(4, 8, -8)
            for s in range(4):
                split_lo(dve, U_GATE + s + 1, 4, 0)
                if s == 1:
                    nsa_weights(dve, ca, 6)
                if s == 2:
                    nsa_weights(dve, cb, 7)
                done(dve, U_GATE + s, 4, 0)
                evac(dve, U_GATE + s, 4, 0, G[:, (12 + s) * T:(13 + s) * T])
                if s == 0:
                    nsa_softmax(dve, ca, 6)
                if s == 1:
                    nsa_copy_d(dve, 6)
                    nsa_softmax(dve, cb, 7)
                if s == 2:
                    nsa_out_lo(dve, 6)
                    nsa_copy_d(dve, 7)
                if s == 3:
                    nsa_out_lo(dve, 7)
            with dve.Fori(1, 5) as i:
                for s in range(4):
                    split_lo(dve, U_GATE + s + 1, 4, i)
                    done(dve, U_GATE + s, 4, i)
                    evac(dve, U_GATE + s, 4, i, G[:, bass.ds((12 + s) * T + 4 * T * i, T)])

            with dve.Fori(0, 4) as i:
                for s in range(4):
                    U, j = U_UP + s, 4 * i + s
                    split_lo(dve, U + 1, 4, i)
                    dve.wait_ge(up_sg, j + 1)
                    done(dve, U, 4, i)
                    dve.tensor_tensor(up_t, psU[U % 2][:, :].rearrange("p (a n) -> p a n", a=2),
                                      gates(j), ALU.mult).then_inc(evacuated, 1)
                    dve.wait_ge(evacuated, U + 4 * i + 1)
                    dve.tensor_tensor(up_m, up_t[:, 0], up_t[:, 1], ALU.add).then_inc(up_mr, 1)
                    dve.wait_ge(up_hi, j + 1)
                    dve.tensor_tensor(ch(AL, j, T), up_m, ch(AH, j, T), ALU.subtract).then_inc(up_lo, 1)

            def add_to_x(U, i, kc):
                done(dve, U, 4, i)
                dve.tensor_tensor(ch(X, kc, T), psU[U % 2][:, 0:T], ch(X, kc, T), ALU.add)\
                   .then_inc(evacuated, 1)

            with dve.Fori(0, 4) as i:
                for s in range(4):
                    U, kc = U_OUT + s, 4 * i + s
                    split_lo(dve, U + 1, 4, i)
                    add_to_x(U, i, kc)
                    dve_chunk(dve, 16 + s + 4 * i, kc, V_FFN, BH, BL, T)
            for (h0, n_h), (ug, ud) in zip(PASSES, u_ffn):
                def hidden(i, norm=False):
                    for s in range(2):
                        Ug, n = ug + 2 * s, h0 + s + 2 * i
                        split_lo(dve, Ug + 1, 4, i)
                        if norm and s == 0:
                            dve_norm(dve, 1, T)
                        done(dve, Ug, 4, i)
                        evac(dve, Ug, 4, i, gsl[:, s])
                        split_lo(dve, Ug + 2, 4, i)
                        done(dve, Ug + 1, 4, i)
                        evac(dve, Ug + 1, 4, i, hup)
                        dve.wait_ge(evacuated, Ug + 2 + 4 * i)
                        dve.wait_ge(ff_silu, n + 1)
                        dve.tensor_tensor(hpr, gsl[:, s], hup, ALU.mult).then_inc(ff_h, 1)
                        dve.wait_ge(ff_hi, n + 1)
                        dve.tensor_tensor(ch(AL, 2 * i + s, T), hpr, ch(AH, 2 * i + s, T), ALU.subtract)\
                           .then_inc(ff_lo, 1)
                if h0 == 0:
                    hidden(0, True)
                    with dve.Fori(1, n_h // 2) as i:
                        hidden(i)
                else:
                    with dve.Fori(0, n_h // 2) as i:
                        hidden(i)
                with dve.Fori(0, 4) as i:
                    for s in range(4):
                        U, kc = ud + s, 4 * i + s
                        split_lo(dve, U + 1, 4, i)
                        add_to_x(U, i, kc)
                        if h0 == PASSES[-1][0]:
                            dve_chunk(dve, 32 + s + 4 * i, kc, V_PRE, BH, BL, TM)
            dve_second(dve)
            for n in range(8):
                for t in range(2):
                    k = 2 * n + t
                    dve.wait_ge(o_t, k + 1)
                    dve.tensor_copy(otok[:, t, 2 * n * P:2 * (n + 1) * P], x_banks[k % 4][:, 0:T])\
                       .then_inc(o_c, 1)

        @block.gpsimd
        def _(pool):
            for kc in range(KC):
                pool_square(pool, kc, kc % 2, T, kc == 0)
            pool.wait_ge(c_x, KC)
            for m in range(3):
                cmp_load(pool, m)
            pool.wait_ge(evacuated, U_NKV + 2)
            cmp_windows(pool, kraw, V_PEK, P, cpk)
            pool.wait_ge(evacuated, U_NKV + 3)
            cmp_windows(pool, ktraw, V_PET, 64, cpt)
            pool.wait_ge(evacuated, U_NKV + 5)
            cmp_windows(pool, vraw, V_PEV, P, cpv)
            for m in range(3, len(CPIECES)):
                cmp_load(pool, m)
            pool.wait_ge(nk_v, 4)
            pool.wait_ge(cm_kcr, 1)

            def group(i, g):
                if not isinstance(i, int) or i > 1:
                    pool.wait_ge(na_olo, 2 * i - 2)
                for dst, src in ((vs_c, vs_t), (vw_c, vw_t)):
                    pool.tensor_copy(dst, src[:, bass.ds(g, 1)].rearrange("p a t d -> p (a t) d"))
                pool.tensor_copy(vc_c, vc_t[:, bass.ds(g, 1)].rearrange("p a d -> p (a d)"))\
                    .then_inc(na_vc, 1)

            group(1, 0)
            with pool.Fori(2, 5) as i:
                group(i, (i - 1) // 2)

            def squares(c0, N, first):
                for s in range(4):
                    pool_square(pool, c0 + s, s % 2, N, first and s == 0)

            squares(16, T, True)
            with pool.Fori(1, 4) as i:
                squares(16 + 4 * i, T, False)
            squares(32, TM, True)
            with pool.Fori(1, 4) as i:
                squares(32 + 4 * i, TM, False)
            pool_second(pool)


_INS = ["x", "norm_attn", "w_in", "fox_f_bias", "fox_q_gain", "fox_k_gain", "nsa_q_gain",
        "nsa_kc_gain", "nsa_ks_gain", "nsa_kw_gain", "cmp_pe_k", "cmp_w1_k", "cmp_w2_k", "cmp_pe_v",
        "cmp_w1_v", "cmp_w2_v", "w_up_fox", "w_up_nsa", "w_out", "norm_ffn", "w_ffn_gate",
        "w_ffn_up", "w_ffn_down", "meta_tokens_2", "pre_norm_2", "post_norm_2", "attn_w_in_2",
        "attn_q_norm_2", "attn_k_norm_2", "attn_w_out_2", "gla_w_in_2", "gla_gk_up_2",
        "gla_gk_bias_2", "gla_o_norm_2", "gla_w_out_2"]


def kernel(**inputs):
    import concourse.bacc as bacc
    from concourse.bass_utils import run_bass_kernel_spmd

    nc = bacc.Bacc("TRN2", target_bir_lowering=False, num_devices=1, dynamic_dma_scratch_size=SCRATCH)
    arrays, aps = {}, {}
    for name in _INS + ["const"]:
        v = np.ascontiguousarray(shape_constants() if name == "const" else inputs[name])
        arrays["in_" + name] = v
        aps[name] = nc.dram_tensor("in_" + name, v.shape, mybir.dt.from_np(v.dtype),
                                   kind="ExternalInput").ap()
    out = nc.dram_tensor("out", (1, T, D), F32, kind="ExternalOutput").ap()
    program(nc, aps, aps["const"], out.rearrange("a t d -> (a t) d"))
    r = run_bass_kernel_spmd(nc, [arrays], core_ids=[0])
    return r.results[0]["out"]
```
